# Optimizing a Trainium2 kernel written in Bass

```python
import jax, jax.numpy as jnp
from jax import lax
import numpy as np

D_MODEL = 1024
BATCH = 1
SEQ = 512
DEPTH = 2
DEC_BATCH = 8
DEC_SEQ = 4
PAST_LEN = 4096
PAGE_SIZE = 128

D_FF = 2816
ML_HEADS = 4
ML_DK = 128
ML_DV = D_MODEL // ML_HEADS
GLA_HEADS = 4
GLA_DK = 128
GLA_DV = D_MODEL // GLA_HEADS
GLA_RANK = 16
GLA_TAU = 16.0
LRU_WIDTH = D_MODEL
LRU_BLOCKS = 8
LRU_BW = LRU_WIDTH // LRU_BLOCKS
LRU_C = 8.0
CONV_W = 4
CHUNK = 64
N_BRANCH = 3
EPS = 1e-6
ML_QK = ML_HEADS * ML_DK
GLA_QK = GLA_HEADS * GLA_DK
SPLITS = (ML_QK, ML_QK, D_MODEL, D_MODEL, 2 * ML_HEADS, GLA_QK, GLA_QK, D_MODEL, D_MODEL, GLA_RANK, LRU_WIDTH, LRU_WIDTH, N_BRANCH * D_MODEL)
D_IN = ML_QK * 2 + D_MODEL * 2 + 2 * ML_HEADS + GLA_QK * 2 + D_MODEL * 2 + GLA_RANK + LRU_WIDTH * 2 + N_BRANCH * D_MODEL

kernel_name = 'hybrid_mlstm_gla_rglru_macaron_step'

F32 = jnp.float32

def _rmsnorm(x, g):
    xf = x.astype(F32)
    y = xf * lax.rsqrt(jnp.mean(xf * xf, axis=-1, keepdims=True) + EPS)
    return (y * g.astype(F32)).astype(x.dtype)

def _swiglu(xn, w_in, w_out):
    gu = xn @ w_in
    g, u = gu[..., :D_FF], gu[..., D_FF:]
    return (jax.nn.silu(g) * u) @ w_out

def _split_cols(a):
    return jnp.split(a, np.cumsum(SPLITS)[:-1].tolist(), axis=-1)

def _heads(a, n):
    B, T, _ = a.shape
    return a.reshape(B, T, n, -1).transpose(0, 2, 1, 3)

def _chunk_len(T):
    return CHUNK if T % CHUNK == 0 else T

def _head_layernorm(h, g):
    B, H, T, d = h.shape
    h = h.transpose(0, 2, 1, 3)
    mu = jnp.mean(h, axis=-1, keepdims=True)
    hc = h - mu
    h = hc * lax.rsqrt(jnp.mean(hc * hc, axis=-1, keepdims=True) + EPS)
    return h.reshape(B, T, H * d) * g.astype(F32)

def _head_rmsnorm(h, g):
    B, H, T, d = h.shape
    h = h.transpose(0, 2, 1, 3)
    h = h * lax.rsqrt(jnp.mean(h * h, axis=-1, keepdims=True) + EPS)
    return h.reshape(B, T, H * d) * g.astype(F32)

def _mlstm(q, k, v, log_i, log_f, C0, n0, m0):
    B, H, T, _ = q.shape
    L = _chunk_len(T)
    nc = T // L
    causal = jnp.tril(jnp.ones((L, L), dtype=bool))

    def to_chunks(a):
        return jnp.moveaxis(a.reshape(B, H, nc, L, *a.shape[3:]), 2, 0)

    def step(carry, inp):
        C, n, m = carry
        qc, kc, vc, ic, fc = inp
        b = jnp.cumsum(fc, axis=-1)
        D = jnp.where(causal, b[..., :, None] - b[..., None, :] + ic[..., None, :], -jnp.inf)
        m_inter = b + m[..., None]
        m_t = jnp.maximum(m_inter, jnp.max(D, axis=-1))
        s_inter = jnp.exp(m_inter - m_t)
        w = jnp.einsum('bhtd,bhsd->bhts', qc, kc) * jnp.exp(D - m_t[..., None])
        num = jnp.einsum('bhts,bhsv->bhtv', w, vc) + s_inter[..., None] * jnp.einsum('bhvd,bhtd->bhtv', C, qc)
        den = jnp.sum(w, axis=-1) + s_inter * jnp.einsum('bhd,bhtd->bht', n, qc)
        h = num / jnp.maximum(jnp.abs(den), jnp.exp(-m_t))[..., None]
        g = b[..., -1:] - b + ic
        m_new = jnp.maximum(b[..., -1] + m, jnp.max(g, axis=-1))
        wk = jnp.exp(g - m_new[..., None])
        decay = jnp.exp(b[..., -1] + m - m_new)
        C_new = decay[..., None, None] * C + jnp.einsum('bhsv,bhsd->bhvd', vc * wk[..., None], kc)
        n_new = decay[..., None] * n + jnp.einsum('bhs,bhsd->bhd', wk, kc)
        return (C_new, n_new, m_new), h

    carry0 = (C0.astype(F32), n0.astype(F32), m0.astype(F32))
    xs = (to_chunks(q), to_chunks(k), to_chunks(v), to_chunks(log_i), to_chunks(log_f))
    (C1, n1, m1), h = lax.scan(step, carry0, xs)
    h = jnp.moveaxis(h, 0, 2).reshape(B, H, T, -1)
    return h, C1, n1, m1

def _gla(q, k, v, log_a, S0):
    B, H, T, _ = q.shape
    L = _chunk_len(T)
    nc = T // L
    causal = jnp.tril(jnp.ones((L, L), dtype=bool))

    def to_chunks(a):
        return jnp.moveaxis(a.reshape(B, H, nc, L, *a.shape[3:]), 2, 0)

    def step(S, inp):
        qc, kc, vc, ac = inp
        b = jnp.cumsum(ac, axis=2)
        diff = jnp.where(causal[:, :, None], b[:, :, :, None, :] - b[:, :, None, :, :], -jnp.inf)
        A = jnp.einsum('bhtd,bhsd,bhtsd->bhts', qc, kc, jnp.exp(diff))
        o = jnp.einsum('bhts,bhsv->bhtv', A, vc) + jnp.einsum('bhtd,bhdv->bhtv', qc * jnp.exp(b), S)
        bL = b[:, :, -1]
        S_new = jnp.exp(bL)[..., None] * S + jnp.einsum('bhsd,bhsv->bhdv', kc * jnp.exp(bL[:, :, None] - b), vc)
        return S_new, o

    xs = (to_chunks(q), to_chunks(k), to_chunks(v), to_chunks(log_a))
    S1, o = lax.scan(step, S0.astype(F32), xs)
    o = jnp.moveaxis(o, 0, 2).reshape(B, H, T, -1)
    return o, S1

def _causal_conv(x, buf, w, b):
    T = x.shape[1]
    xp = jnp.concatenate([buf.astype(x.dtype), x], axis=1)
    y = b + sum(xp[:, j:j + T] * w[j] for j in range(CONV_W))
    return y, xp[:, -(CONV_W - 1):]

def _rglru(xc, w_a, b_a, w_i, b_i, lam, h0, pos):
    B, T, C = xc.shape
    xb = xc.reshape(B, T, LRU_BLOCKS, LRU_BW)
    r = jax.nn.sigmoid(jnp.einsum('btnc,ncd->btnd', xb, w_a.astype(F32)).reshape(B, T, C) + b_a)
    i = jax.nn.sigmoid(jnp.einsum('btnc,ncd->btnd', xb, w_i.astype(F32)).reshape(B, T, C) + b_i)
    log_a = -LRU_C * r * jax.nn.softplus(-lam.astype(F32))
    a = jnp.exp(log_a)
    mult = jnp.sqrt(-jnp.expm1(2.0 * log_a))
    mult = jnp.where((pos == 0)[None, :, None], 1.0, mult)
    u = mult * i * xc
    u = u.at[:, 0].add(a[:, 0] * h0.astype(F32))

    def comb(l, rr):
        return (l[0] * rr[0], rr[0] * l[1] + rr[1])

    _, h = lax.associative_scan(comb, (a, u), axis=1)
    return h, h[:, -1]

def _layer(x, pos, state, p):
    C0, n0, m0, S0, h0, cb0 = state
    B, T, _ = x.shape
    x = x + 0.5 * _swiglu(_rmsnorm(x, p['norm_ffn1']), p['w_ffn1_in'], p['w_ffn1_out'])
    xn = _rmsnorm(x, p['norm_mix'])
    (mq, mk, mv, mo, mg_if, gq, gk, gv, gg, glr, lx, ly, mgate) = _split_cols(xn @ p['w_in'])
    q = _heads(mq, ML_HEADS).astype(F32)
    k = _heads(mk, ML_HEADS).astype(F32) * (ML_DK ** -0.5)
    v = _heads(mv, ML_HEADS).astype(F32)
    gates = mg_if.astype(F32) + p['b_ml_if'].astype(F32)
    log_i = gates[..., :ML_HEADS].transpose(0, 2, 1)
    log_f = jax.nn.log_sigmoid(gates[..., ML_HEADS:]).transpose(0, 2, 1)
    h_ml, C1, n1, m1 = _mlstm(q, k, v, log_i, log_f, C0, n0, m0)
    y_ml = _head_layernorm(h_ml, p['g_ml_norm']) * jax.nn.sigmoid(mo.astype(F32))
    gq_ = _heads(gq, GLA_HEADS).astype(F32) * (GLA_DK ** -0.5)
    gk_ = _heads(gk, GLA_HEADS).astype(F32)
    gv_ = _heads(gv, GLA_HEADS).astype(F32)
    log_a = jax.nn.log_sigmoid((glr @ p['w_gla_lr2']).astype(F32) + p['b_gla_gate'].astype(F32)) / GLA_TAU
    o_gla, S1 = _gla(gq_, gk_, gv_, _heads(log_a, GLA_HEADS), S0)
    y_gla = _head_rmsnorm(o_gla, p['g_gla_norm']) * jax.nn.silu(gg.astype(F32))
    xc, cb1 = _causal_conv(lx, cb0, p['w_conv'], p['b_conv'])
    h_lru, h1 = _rglru(xc.astype(F32), p['w_lru_a'], p['b_lru_a'].astype(F32), p['w_lru_i'], p['b_lru_i'].astype(F32), p['lru_lambda'], h0, pos)
    y_lru = h_lru * jax.nn.gelu(ly.astype(F32))
    gm = jax.nn.sigmoid(mgate.astype(F32)).reshape(B, T, N_BRANCH, D_MODEL)
    merged = gm[:, :, 0] * y_ml + gm[:, :, 1] * y_gla + gm[:, :, 2] * y_lru
    x = x + merged.astype(x.dtype) @ p['w_out']
    x = x + 0.5 * _swiglu(_rmsnorm(x, p['norm_ffn2']), p['w_ffn2_in'], p['w_ffn2_out'])
    return x, (C1, n1, m1, S1, h1, cb1)

def setup_inputs(seed: int = 0) -> dict:
    key = jax.random.key(seed)
    ks = iter(jax.random.split(key, 48))

    def nrm(shape, s):
        return jax.random.normal(next(ks), shape, F32) * s

    Ld = DEPTH
    d = D_MODEL
    u = jax.random.uniform(next(ks), (Ld, LRU_WIDTH), F32, minval=0.9, maxval=0.999)
    sa = u ** (1.0 / LRU_C)
    lam = jnp.log(sa) - jnp.log1p(-sa)
    b_if = jnp.concatenate([nrm((Ld, ML_HEADS), 0.1), jnp.linspace(3.0, 6.0, ML_HEADS, dtype=F32)[None] + nrm((Ld, ML_HEADS), 0.1)], axis=-1)
    return {
        'x_prompt': nrm((BATCH, SEQ, d), 1.0),
        'x_sample': nrm((DEC_BATCH, DEC_SEQ, d), 1.0),
        'state_mlstm_C': nrm((Ld, DEC_BATCH, ML_HEADS, ML_DV, ML_DK), 0.05),
        'state_mlstm_n': jnp.abs(nrm((Ld, DEC_BATCH, ML_HEADS, ML_DK), 0.5)),
        'state_mlstm_m': nrm((Ld, DEC_BATCH, ML_HEADS), 1.0),
        'state_gla_S': nrm((Ld, DEC_BATCH, GLA_HEADS, GLA_DK, GLA_DV), 0.5),
        'state_lru_h': nrm((Ld, DEC_BATCH, LRU_WIDTH), 0.5),
        'state_lru_conv': nrm((Ld, DEC_BATCH, CONV_W - 1, LRU_WIDTH), 1.0),
        'norm_ffn1': 1.0 + nrm((Ld, d), 0.02),
        'w_ffn1_in': nrm((Ld, d, 2 * D_FF), d ** -0.5),
        'w_ffn1_out': nrm((Ld, D_FF, d), D_FF ** -0.5),
        'norm_mix': 1.0 + nrm((Ld, d), 0.02),
        'w_in': nrm((Ld, d, D_IN), d ** -0.5),
        'b_ml_if': b_if,
        'g_ml_norm': 1.0 + nrm((Ld, D_MODEL), 0.02),
        'w_gla_lr2': nrm((Ld, GLA_RANK, GLA_QK), GLA_RANK ** -0.5),
        'b_gla_gate': nrm((Ld, GLA_QK), 0.1),
        'g_gla_norm': 1.0 + nrm((Ld, D_MODEL), 0.02),
        'w_conv': nrm((Ld, CONV_W, LRU_WIDTH), CONV_W ** -0.5),
        'b_conv': nrm((Ld, LRU_WIDTH), 0.02),
        'w_lru_a': nrm((Ld, LRU_BLOCKS, LRU_BW, LRU_BW), LRU_BW ** -0.5),
        'b_lru_a': nrm((Ld, LRU_WIDTH), 0.1),
        'w_lru_i': nrm((Ld, LRU_BLOCKS, LRU_BW, LRU_BW), LRU_BW ** -0.5),
        'b_lru_i': nrm((Ld, LRU_WIDTH), 0.1),
        'lru_lambda': lam,
        'w_out': nrm((Ld, d, d), d ** -0.5),
        'norm_ffn2': 1.0 + nrm((Ld, d), 0.02),
        'w_ffn2_in': nrm((Ld, d, 2 * D_FF), d ** -0.5),
        'w_ffn2_out': nrm((Ld, D_FF, d), D_FF ** -0.5),
        'norm_final': 1.0 + nrm((d,), 0.02),
    }

def reference(x_prompt, x_sample, state_mlstm_C, state_mlstm_n, state_mlstm_m, state_gla_S, state_lru_h, state_lru_conv,
              norm_ffn1, w_ffn1_in, w_ffn1_out, norm_mix, w_in, b_ml_if, g_ml_norm, w_gla_lr2, b_gla_gate, g_gla_norm,
              w_conv, b_conv, w_lru_a, b_lru_a, w_lru_i, b_lru_i, lru_lambda, w_out, norm_ffn2, w_ffn2_in, w_ffn2_out,
              norm_final):
    Bp, Tp, _ = x_prompt.shape
    Ts = x_sample.shape[1]
    pos_p = jnp.arange(Tp)
    pos_s = PAST_LEN + jnp.arange(Ts)
    zero_p = (jnp.zeros((Bp, ML_HEADS, ML_DV, ML_DK), F32), jnp.zeros((Bp, ML_HEADS, ML_DK), F32),
              jnp.zeros((Bp, ML_HEADS), F32), jnp.zeros((Bp, GLA_HEADS, GLA_DK, GLA_DV), F32),
              jnp.zeros((Bp, LRU_WIDTH), F32), jnp.zeros((Bp, CONV_W - 1, LRU_WIDTH), x_prompt.dtype))
    yp, ys = x_prompt, x_sample
    new_p, new_s = [], []
    for l in range(DEPTH):
        p = {'norm_ffn1': norm_ffn1[l], 'w_ffn1_in': w_ffn1_in[l], 'w_ffn1_out': w_ffn1_out[l],
             'norm_mix': norm_mix[l], 'w_in': w_in[l], 'b_ml_if': b_ml_if[l], 'g_ml_norm': g_ml_norm[l],
             'w_gla_lr2': w_gla_lr2[l], 'b_gla_gate': b_gla_gate[l], 'g_gla_norm': g_gla_norm[l],
             'w_conv': w_conv[l], 'b_conv': b_conv[l], 'w_lru_a': w_lru_a[l], 'b_lru_a': b_lru_a[l],
             'w_lru_i': w_lru_i[l], 'b_lru_i': b_lru_i[l], 'lru_lambda': lru_lambda[l], 'w_out': w_out[l],
             'norm_ffn2': norm_ffn2[l], 'w_ffn2_in': w_ffn2_in[l], 'w_ffn2_out': w_ffn2_out[l]}
        yp, st_p = _layer(yp, pos_p, zero_p, p)
        st_in = (state_mlstm_C[l], state_mlstm_n[l], state_mlstm_m[l], state_gla_S[l], state_lru_h[l], state_lru_conv[l])
        ys, st_s = _layer(ys, pos_s, st_in, p)
        new_p.append(st_p)
        new_s.append(st_s)
    y_prompt = _rmsnorm(yp, norm_final)
    y_sample = _rmsnorm(ys, norm_final)
    p_C = jnp.stack([s[0] for s in new_p])
    p_n = jnp.stack([s[1] for s in new_p])
    p_m = jnp.stack([s[2] for s in new_p])
    p_S = jnp.stack([s[3] for s in new_p])
    p_h = jnp.stack([s[4] for s in new_p])
    p_conv = jnp.stack([s[5] for s in new_p])
    s_C = jnp.stack([s[0] for s in new_s])
    s_n = jnp.stack([s[1] for s in new_s])
    s_m = jnp.stack([s[2] for s in new_s])
    s_S = jnp.stack([s[3] for s in new_s])
    s_h = jnp.stack([s[4] for s in new_s])
    s_conv = jnp.stack([s[5] for s in new_s])
    return (y_prompt, y_sample, p_C, p_n, p_m, p_S, p_h, p_conv, s_C, s_n, s_m, s_S, s_h, s_conv)


_drawn_inputs = setup_inputs


def setup_inputs(seed=0):
    import zlib

    import numpy as np

    out = dict(_drawn_inputs(seed))
    spreads = {}
    factors = {'norm_ffn1': 3.041,
     'g_ml_norm': 19.016,
     'g_gla_norm': 18.957,
     'norm_ffn2': 4.892,
     'norm_final': 7.595}
    for name, (base, spread) in spreads.items():
        noise = np.random.default_rng([zlib.crc32(name.encode()), seed]).standard_normal(out[name].shape)
        drawn = base * np.exp(spread * noise) if base else spread * noise
        out[name] = __import__('jax').numpy.asarray(drawn.astype(out[name].dtype))
    for name, factor in factors.items():
        out[name] = (out[name] * factor).astype(out[name].dtype)
    return out
```

```python
from contextlib import ExitStack

import concourse.bass as bass
from concourse import mybir

F32 = mybir.dt.float32
F32R = mybir.dt.float32r
I32 = mybir.dt.int32
ALU = mybir.AluOpType
ACT = mybir.ActivationFunctionType
ds = bass.ds

P = 128
D = 1024
KT = D // P
DEPTH = 2
T = 512
SEQS, TS = 8, 4
NS = SEQS * TS
N = T + NS
HALF = N // 2
FF = 2816
HEADS = 4
DK = 128
DV = D // HEADS
C = 128
NC = T // C
EPS = 1e-6
NEG = -1e30
LEVELS = [64, 32, 16, 8, 4, 2, 1]
NL = len(LEVELS)
NLS = 2

FF_HALVES = [12, 10]
assert sum(FF_HALVES) * P == FF
W_SLOT = 2048

FFN_BLOCKS = sum(FF_HALVES) + 2 * KT
FFN_TILES = 2 * sum(FF_HALVES) + 2 * KT
HEAD_BLOCKS, HEAD_TILES = 4, 8
LRU_BLOCKS, LRU_TILES = 3, 6
MIX_BLOCKS = 2 * HEADS * HEAD_BLOCKS + KT // 2 * LRU_BLOCKS
GATE_TILES = 2
MIX_TILES = GATE_TILES + 2 * HEADS * HEAD_TILES + KT // 2 * LRU_TILES
OUT_BLOCKS, OUT_TILES = KT // 2, KT
BLK_MIX = FFN_BLOCKS
BLK_OUT = BLK_MIX + MIX_BLOCKS
BLK_FFN2 = BLK_OUT + OUT_BLOCKS
LAYER_BLOCKS = BLK_FFN2 + FFN_BLOCKS
TILE_MIX = FFN_TILES
TILE_OUT = TILE_MIX + MIX_TILES
TILE_FFN2 = TILE_OUT + OUT_TILES
LAYER_TILES = TILE_FFN2 + FFN_TILES

V_MIX, V_FFN2, V_NEXT, V_GML, V_GGLA = 0, 8, 16, 24, 32
V_CONV, V_BCONV, V_BA, V_BI, V_LAM, V_BGLA = 40, 72, 80, 88, 96, 104
V_COLS = 108
V_FIRST = DEPTH * V_COLS
V_ALL = V_FIRST + KT
GATE_W = KT * P
STORES = 2 + HEADS * 3 + HEADS * 2 + 4


def spread(ap, dim, n):
    shape = list(ap.shape)
    shape[dim] = n
    return ap.broadcast_to(shape)


class Chain:

    def __init__(self, eng, sem, ready):
        self.eng, self.sem, self.ready, self.n = eng, sem, ready, 0
        self.spare = eng.alloc_register(f"{sem.name}_spare")
        eng.reg_mov(self.spare, 1)

    def hold(self):
        self.eng.reg_alu(self.spare, self.spare, 1, ALU.max)

    def end(self):
        self.eng.wait_ge(self.ready, self.spare)

    def restart(self):
        self.hold()
        self.eng.sem_clear(self.sem)
        self.n = 0

    def link(self, ins):
        self.n += 1
        ins.then_inc(self.sem, 1)
        self.eng.wait_ge(self.sem, self.n)


CONST_LOADS = 10


def trunk(nc, x_T, w_up1, w_down1, w_mix, w_gates, w_o, w_up2, w_down2, vec, b_if, w_lr2, w_ra, w_ri, consts, level_masks,
          m0, c0, n0, s0, h0, conv0, o_y, o_pc, o_pm, o_ps, o_ph, o_pconv,
          o_sc, o_sn, o_sm, o_ss, o_sh, o_sconv, rows_dram):
    with ExitStack() as ctx:
        def sb(name, shape, dt=F32, where=ctx):
            return where.enter_context(nc.sbuf_tensor(name, shape, dt))

        def sem(name):
            return ctx.enter_context(nc.semaphore(name))

        x = sb("x", [P, KT, N])
        xh = sb("xh", [P, KT, N], F32R)
        xl = sb("xl", [P, KT, N], F32R)
        stage = sb("stage", [P, 2, W_SLOT])
        wh = sb("wh", [P, 2, W_SLOT], F32R)
        wl = sb("wl", [P, 2, W_SLOT], F32R)
        gstage = sb("gstage", [P, GATE_W])
        V = sb("vectors", [P, V_ALL])
        ones = sb("ones", [P, P])
        ident = sb("ident", [P, P])
        eps_t = sb("eps_t", [P, 1])
        one_t = sb("one_t", [P, 1])
        acc = sb("acc", [P, N])
        sq = sb("sq", [P, N])
        xg = sb("xg", [P, N])
        sd = sb("sd", [P, N])
        rstd = sb("rstd", [P, N])
        sdT = sb("sdT", [P, 5])
        rstdT = sb("rstdT", [P, 5])
        c8 = sb("c8", [P, DEPTH * KT])
        nc8 = sb("nc8", [P, DEPTH * KT])
        masks = sb("masks", [P, NL, P], I32)
        neg_p = sb("neg_p", [P, P])
        neg_s = sb("neg_s", [NS, NS])
        seqm = sb("seqm", [NS, SEQS])
        reset = sb("reset", [P, N])
        bif = sb("bif", [HEADS, DEPTH, 2])
        m0t = sb("m0t", [HEADS, DEPTH, SEQS])
        t8 = sb("t8", [P, SEQS])
        m_out = sb("m_out", [HEADS, 1 + SEQS])
        ff = ExitStack()
        hh = sb("hh", [P, FF_HALVES[0], N], F32R, ff)
        hl = sb("hl", [P, FF_HALVES[0], N], F32R, ff)
        gs = sb("gs", [P, N], where=ff)
        us = sb("us", [P, N], where=ff)
        sg = sb("sg", [P, N], where=ff)
        hp = sb("hp", [P, N], where=ff)
        ff.close()
        merged = sb("merged", [P, KT, N])
        heads = ExitStack()
        gwh = sb("gwh", [P, GATE_W], F32R, heads)
        gwl = sb("gwl", [P, GATE_W], F32R, heads)
        heads.close()
        heads = ExitStack()
        qT = sb("qT", [P, N], where=heads)
        kT = sb("kT", [P, N], where=heads)
        qs = sb("qs", [P, N], where=heads)
        val = sb("val", [P, NC + 1, DV + P], where=heads)
        seven = sb("seven", [P, NL, N], where=heads)
        wS = sb("wS", [P, N], where=heads)
        Kw = sb("Kw", [P, NC, P], where=heads)
        Kts = sb("Kts", [NS, P], where=heads)
        Kws = sb("Kws", [NS, SEQS, P], where=heads)
        Cst = sb("Cst", [P, NC, DV + P], where=heads)
        CS = sb("CS", [P, SEQS, DV], where=heads)
        nS = sb("nS", [P, 2, SEQS], where=heads)
        nB = sb("nB", [P, SEQS, P], where=heads)
        Hh = sb("Hh", [P, 2, N], where=heads)
        Gm = sb("Gm", [P, 2, N], where=heads)
        tg = sb("tg", [P, N], where=heads)
        cols = sb("cols", [P, 8], where=heads)
        lr2 = sb("lr2", [P, P], where=heads)
        heads.close()
        lru = ExitStack()
        mh = sb("mh", [P, KT, N], F32R, lru)
        ml = sb("ml", [P, KT, N], F32R, lru)
        lxp = sb("lxp", [P, 2, T + 3], where=lru)
        lxs = sb("lxs", [P, 2, SEQS, TS + 3], where=lru)
        xc = sb("xc", [P, N], where=lru)
        rr = sb("rr", [P, N], where=lru)
        ii = sb("ii", [P, N], where=lru)
        aa = sb("aa", [P, N], where=lru)
        tt = sb("tt", [P, N], where=lru)
        hseq = sb("hseq", [P, 2, N], where=lru)
        lyg = sb("lyg", [P, 2, N], where=lru)
        wra = sb("wra", [P, KT // 2, P], where=lru)
        wri = sb("wri", [P, KT // 2, P], where=lru)
        h0t = sb("h0t", [P, KT, SEQS], where=lru)
        cv0 = sb("cv0", [P, KT, SEQS, 3], where=lru)
        ph = sb("ph", [P, KT], where=lru)
        sh = sb("sh", [P, KT, SEQS], where=lru)
        pcv = sb("pcv", [P, KT, 3], where=lru)
        scv = sb("scv", [P, KT, SEQS, 3], where=lru)
        lru.close()

        def psum(name, shape):
            return ctx.enter_context(nc.psum_tensor(name, shape, F32))

        pair = [psum("stream_a", [P, 2, 512]), psum("stream_b", [P, 2, 512])]
        Q = psum("mix", [P, 4, 512])

        const_loaded = sem("const_loaded")
        x_loaded = sem("x_loaded")
        block_loaded = [sem("block_loaded_0"), sem("block_loaded_1")]
        split_done = sem("split_done")
        tile_done = sem("tile_done")
        tile_free = sem("tile_free")
        silu_done = sem("silu_done")
        h_done = sem("h_done")
        sq_ready = sem("sq_ready")
        acc_ready = sem("acc_ready")
        norm_sum = sem("norm_sum")
        sd_ready = sem("sd_ready")
        c8_ready = sem("c8_ready")
        c8_in = sem("c8_in")
        gate_loaded = sem("gate_loaded")
        gate_split = sem("gate_split")
        gate_in = sem("gate_in")
        gate_ln = sem("gate_ln")
        rows_ready = sem("rows_ready")
        rows_stored = sem("rows_stored")
        head_done = sem("head_done")
        state_stored = sem("state_stored")
        gate_act = sem("gate_act")
        dve_chain, act_chain, pool_chain = sem("dve_chain"), sem("act_chain"), sem("pool_chain")
        init_done = sem("init_done")
        a_rows = sem("a_rows_loaded")
        a_cs = sem("a_state_loaded")
        a_si, a_exin, a_ex = sem("a_si"), sem("a_exp_in"), sem("a_exp")
        a_scores, a_kw, a_u, a_c = sem("a_scores"), sem("a_weights"), sem("a_update"), sem("a_state")
        a_out, a_h, a_us, a_csd = sem("a_out"), sem("a_h"), sem("a_sample_update"), sem("a_sample_state")
        a_mean, a_hc, a_sq, a_sqs = sem("a_mean"), sem("a_centred"), sem("a_squares"), sem("a_square_sum")
        a_var, a_sd = sem("a_var"), sem("a_sd")
        b_lr, b_cs = sem("b_lr_loaded"), sem("b_state_loaded")
        b_z, b_zin, b_ln, b_diff, b_exp = sem("b_z"), sem("b_z_in"), sem("b_ln"), sem("b_diff"), sem("b_exp")
        b_fac, b_ring, b_took = sem("b_factors"), sem("b_ring_full"), sem("b_ring_took")
        b_u, b_c, b_out, b_h = sem("b_update"), sem("b_state"), sem("b_out"), sem("b_h")
        b_us, b_csd, b_sq, b_sqs = sem("b_sample_update"), sem("b_sample_state"), sem("b_squares"), sem("b_square_sum")
        b_var, b_sd = sem("b_var"), sem("b_sd")
        l_vec, l_w = sem("l_vectors_loaded"), sem("l_weights_loaded")
        l_xc, l_ri, l_sig, l_at, l_min, l_mult = (sem("l_conv"), sem("l_gates"), sem("l_sigmoids"), sem("l_decay"),
                                                  sem("l_mult_in"), sem("l_mult"))
        l_act = sem("l_act")
        m_ready = sem("m_ready")
        lru_done = sem("lru_done")
        y_ready = sem("y_ready")
        y_stored = sem("y_stored")

        RB, SI, EM, Ex = seven[:, 0:4, :], seven[:, 4, :], seven[:, 5, :], seven[:, 6, :]
        glr = xg[64:80, :]
        kh, bc, eb = sq, acc, sd

        def halves(ap):
            return ap.rearrange("p (a b) -> p a b", a=2)

        def banks(p):
            return p[:, :, 0:HALF]

        block = ctx.enter_context(nc.Block())

        @block.sync
        def _(sp):
            sp.dma_start(V[:], vec).then_inc(const_loaded, 16)
            sp.dma_start(x[:], x_T).then_inc(x_loaded, 16)

            def load(n, slot, src):
                sp.wait_ge(split_done, n + 1)
                width = src.shape[1]
                sp.dma_start(stage[:, slot, 0:width], src).then_inc(block_loaded[slot], 16)

            def ffn(L, first, w_up, w_down):
                n = L * LAYER_BLOCKS + first
                up = down = 0
                for tiles in FF_HALVES:
                    with sp.Fori(0, tiles // 2) as i:
                        for j in range(2):
                            load(i * 2 + (n + j), j, w_up[L, i * 2 + (up + j)])
                    n = n + tiles
                    up += tiles
                    with sp.Fori(0, KT // 2) as i:
                        for j in range(2):
                            load(i * 2 + (n + j), j, w_down[L, i * 2 + (down + j), :, 0:tiles * P])
                    n = n + KT
                    down += KT

            sp.wait_ge(init_done, 1)
            with sp.Fori(0, DEPTH) as L:
                ffn(L, 0, w_up1, w_down1)
                sp.dma_start(gstage[:], w_gates[L]).then_inc(gate_loaded, 16)
                with sp.Fori(0, MIX_BLOCKS // 2) as i:
                    for j in range(2):
                        load(L * LAYER_BLOCKS + i * 2 + (BLK_MIX + j), j, w_mix[L, i * 2 + j])
                with sp.Fori(0, OUT_BLOCKS // 2) as i:
                    for j in range(2):
                        load(L * LAYER_BLOCKS + i * 2 + (BLK_OUT + j), j, w_o[L, i * 2 + j])
                ffn(L, BLK_FFN2, w_up2, w_down2)
            for m in range(KT):
                sp.wait_ge(y_ready, m + 1)
                sp.dma_start(o_y[:, m, :], x[:, m, :]).then_inc(y_stored, 16)
            sp.wait_ge(y_stored, 16 * KT)
            sp.wait_ge(state_stored, 16 * DEPTH * STORES)

        @block.gpsimd
        def _(pool):
            chain = Chain(pool, pool_chain, init_done)
            pool.memset(eps_t[:], EPS)
            pool.memset(one_t[:], 1.0).then_inc(split_done, 2)
            pool.memset(rstdT[:], 1.0).then_inc(tile_done, 2)
            pool.memset(sdT[:], 1.0).then_inc(init_done, 1)

            def split(half_n, through, slot, width):
                pool.wait_ge(block_loaded[slot], half_n * 16 + 16)
                pool.wait_ge(tile_done, through + 2)
                chain.hold()
                chain.link(pool.tensor_copy(wh[:, slot, 0:width], stage[:, slot, 0:width]))
                pool.tensor_tensor(wl[:, slot, 0:width], stage[:, slot, 0:width],
                                   wh[:, slot, 0:width].bitcast(F32), ALU.subtract).then_inc(split_done, 1)

            def run(L, first, blocks, width, first_tile, tiles_each, ahead, before=None):
                half = L * (LAYER_BLOCKS // 2) + first // 2
                t = L * LAYER_TILES + first_tile
                last = t if before is None else L * LAYER_TILES + before
                chain.restart()
                split(half, last - ahead, 0, width)
                split(half, last, 1, width)
                with pool.Fori(1, blocks // 2) as i:
                    chain.restart()
                    for j in range(2):
                        split(half + i, t + (i * 2 + (j - 1)) * tiles_each, j, width)

            def ffn(L, first, first_tile, ahead):
                for tiles in FF_HALVES:
                    run(L, first, tiles, 2 * D, first_tile, 2, ahead)
                    run(L, first + tiles, KT, tiles * P, first_tile + 2 * tiles, 1, 2)
                    ahead = 1
                    first += tiles + KT
                    first_tile += 2 * tiles + KT

            pool.wait_ge(init_done, 1)
            with pool.Fori(0, DEPTH) as L:
                ffn(L, 0, 0, 1)
                pool.wait_ge(gate_loaded, L * 16 + 16)
                pool.wait_ge(tile_done, L * LAYER_TILES + FFN_TILES + 2)
                chain.restart()
                chain.link(pool.tensor_copy(gwh[:], gstage[:]))
                pool.tensor_tensor(gwl[:], gstage[:], gwh[:].bitcast(F32), ALU.subtract).then_inc(gate_split, 1)
                run(L, BLK_MIX, MIX_BLOCKS, 2 * D, TILE_MIX + GATE_TILES, 2, 1, before=FFN_TILES)
                run(L, BLK_OUT, OUT_BLOCKS, 2 * D, TILE_OUT, 2, 2)
                ffn(L, BLK_FFN2, TILE_FFN2, 2)
            chain.end()

        @block.tensor
        def _(pe):
            def three_pass(out, lhs, rhs, first, last):
                (lh, ll), (rh, rl) = lhs, rhs
                for a, b, f, z in ((lh, rh, first, False), (ll, rh, False, False), (lh, rl, False, last)):
                    mm = [pe.matmul(out(h), a(h), b(h), start=f, stop=z) for h in range(2)]
                return mm[-1]

            def block_ready(n):
                pe.wait_ge(split_done, n + 3)

            def tile(t, slot, k_tiles, width, col, act=(xh, xl), weights=(wh, wl), late=None, fresh=None,
                     count=1):
                p = pair[slot]
                pe.wait_ge(tile_free, t + 1)
                for k in range(k_tiles):
                    if late and k == k_tiles - 1:
                        late()
                    if fresh is not None:
                        pe.wait_ge(acc_ready, fresh - (k_tiles - 1 - k))
                    c0_ = k * width + col
                    mm = three_pass(lambda h: p[:, h, 0:HALF],
                                    [lambda h, w=w: w[:, c0_:c0_ + P] for w in weights],
                                    [lambda h, a=a: a[:, k, h * HALF:(h + 1) * HALF] for a in act],
                                    k == 0, k == k_tiles - 1)
                mm.then_inc(tile_done, count)

            def norm_squares():
                for h in range(2):
                    mm = pe.matmul(Q[:, h, 0:HALF], ones[:], acc[:, h * HALF:(h + 1) * HALF], start=True, stop=True)
                return mm

            def ffn_in_block(L, n, t, j, norm=None):
                block_ready(n)
                tile(t, 0, KT, 2 * P, 0, weights=(wh[:, j], wl[:, j]), fresh=norm)
                if norm is not None:
                    pe.wait_ge(acc_ready, norm)
                    norm_squares().then_inc(norm_sum, 1)
                tile(t + 1, 1, KT, 2 * P, P, weights=(wh[:, j], wl[:, j]))

            def ffn(L, first, first_tile, h_base, norm):
                n = L * LAYER_BLOCKS + first
                t = L * LAYER_TILES + first_tile
                hd = L * (2 * sum(FF_HALVES)) + h_base
                for half, tiles in enumerate(FF_HALVES):
                    start = 0
                    if half == 0:
                        for j in range(2):
                            ffn_in_block(L, n + j, t + 2 * j, j, norm if j == 0 else None)
                        start = 1
                    with pe.Fori(start, tiles // 2) as i:
                        for j in range(2):
                            ffn_in_block(L, i * 2 + (n + j), i * 4 + (t + 2 * j), j)
                    n, t, hd = n + tiles, t + 2 * tiles, hd + tiles
                    with pe.Fori(0, KT // 2) as i:
                        for j in range(2):
                            block_ready(i * 2 + (n + j))
                            pe.wait_ge(h_done, hd - 1)
                            tile(i * 2 + (t + j), j, tiles, P, 0, act=(hh, hl), weights=(wh[:, j], wl[:, j]),
                                 late=lambda: pe.wait_ge(h_done, hd))
                    n, t = n + KT, t + KT

            def value_tiles(t, j):
                for which, starts in enumerate(([c * C for c in range(NC)], [N - C])):
                    pe.wait_ge(tile_free, t + which + 1)
                    for c, tok in enumerate(starts):
                        out = pair[which][:, c // 2, c % 2 * DV:(c % 2 + 1) * DV]
                        for k in range(KT):
                            for a, b, f, z in ((xh, wh, k == 0, False), (xl, wh, False, False),
                                               (xh, wl, False, k == KT - 1)):
                                mm = pe.matmul(out, a[:, k, tok:tok + C], b[:, j, k * DV:(k + 1) * DV],
                                               start=f, stop=z)
                    mm.then_inc(tile_done, 1)

            def pair_block(n, t, j, after_first=None):
                block_ready(n)
                tile(t, 0, KT, 2 * P, 0, weights=(wh[:, j], wl[:, j]))
                if after_first:
                    after_first()
                tile(t + 1, 1, KT, 2 * P, P, weights=(wh[:, j], wl[:, j]))

            def gate_block(L):
                pe.wait_ge(gate_split, L + 1)
                tile(L * LAYER_TILES + TILE_MIX, 0, KT, P, 0, weights=(gwh, gwl), count=GATE_TILES,
                     fresh=L * (3 * KT) + 2 * KT)
                pe.wait_ge(acc_ready, L * (3 * KT) + 2 * KT)
                norm_squares()
                for c in range(NC + 1):
                    tok = c * C if c < NC else N - C
                    mm = pe.matmul(Q[:, 2, c:c + 1], acc[:, tok:tok + C], ones[:, 0:1], start=True, stop=True)
                mm.then_inc(norm_sum, 1)

            def sample_states(b_, v, out_col, lhs_of):
                for s_ in range(SEQS):
                    mm = pe.matmul(Q[:, b_, out_col + s_ * TS:out_col + (s_ + 1) * TS], lhs_of(s_, v),
                                   qs[:, T + s_ * TS:T + (s_ + 1) * TS], start=False, stop=s_ == SEQS - 1,
                                   skip_group_check=True)
                return mm

            def sample_updates(done):
                for s_ in range(SEQS):
                    mm = pe.matmul(Q[:, s_ // 2, s_ % 2 * DV:(s_ % 2 + 1) * DV], Kws[:, s_, :],
                                   val[0:NS, NC, 0:DV], start=True, stop=True)
                mm.then_inc(done, 1)

            def column_sum(src, b_, done):
                for h in range(2):
                    mm = pe.matmul(Q[:, b_ + h, 0:HALF], ones[:], src[:, h * HALF:(h + 1) * HALF], start=True, stop=True)
                mm.then_inc(done, 1)

            def mlstm_head(L, i):
                B = L * HEADS + i
                n = L * LAYER_BLOCKS + i * HEAD_BLOCKS + BLK_MIX
                t = L * LAYER_TILES + i * HEAD_TILES + (TILE_MIX + GATE_TILES)
                pair_block(n, t, 0)
                block_ready(n + 1)
                value_tiles(t + 2, 1)
                pe.wait_ge(tile_free, t + 6)
                pe.wait_ge(a_rows, B * 16 + 16)
                pe.wait_ge(head_done, L * (2 * HEADS) + i + 1)
                for c in range(NC):
                    sl = slice(c * C, (c + 1) * C)
                    pe.matmul(Q[:, 0, sl], kT[:, sl], qT[:, sl], start=True, stop=True)
                for c in range(NC):
                    sl = slice(c * C, (c + 1) * C)
                    pe.transpose(Q[:, 1, sl], kT[:, sl], ident[:])
                sm = slice(T, N)
                pe.matmul(Q[0:NS, 2, 0:NS], kT[:, sm], qT[:, sm], start=True, stop=True)
                pe.transpose(Q[0:NS, 2, NS:NS + P], kT[:, sm], ident[:])
                for c in range(NC + 1):
                    m = C if c < NC else NS
                    mm = pe.matmul(Q[0:m, 2, 200 + c:201 + c], RB[0:1, 3, c * C:c * C + m], ones[0:1, 0:1],
                                   start=True, stop=True)
                mm.then_inc(a_scores, 1)

                def update(c):
                    sl = slice(0, DV + P)
                    pe.matmul(Q[:, 3 - c % 2, sl], Kw[:, c, :], val[:, c, sl], start=True, stop=True).then_inc(a_u, 1)

                def updates_01():
                    pe.wait_ge(a_kw, B + 1)
                    update(0)
                    update(1)

                pair_block(n + 2, t + 4, 0, updates_01)
                for c in (2, 3):
                    pe.wait_ge(a_c, B * NC + (c - 1))
                    update(c)

                def outputs():
                    pe.wait_ge(a_c, B * NC + NC)
                    for v in range(3):
                        vs = slice(v * P, (v + 1) * P)
                        for c in range(NC):
                            sl = slice(c * C, (c + 1) * C)
                            pe.matmul(Q[:, v, sl], val[:, c, vs], wS[:, sl], start=True, stop=c == 0)
                            if c:
                                pe.matmul(Q[:, v, sl], Cst[:, c - 1, vs], qs[:, sl], start=False, stop=True)
                    pe.wait_ge(a_cs, B * 32 + 32)
                    for v in range(3):
                        pe.matmul(Q[:, 3, v * NS:(v + 1) * NS], val[0:NS, NC, v * P:(v + 1) * P], wS[0:NS, sm],
                                  start=True, stop=False, skip_group_check=True)
                        sample_states(3, v, v * NS, lambda s_, v_: CS[:, s_, v_ * P:(v_ + 1) * P] if v_ < 2
                                      else nB[:, s_, :])
                    pe.matmul(Q[:, 3, 3 * NS:3 * NS + SEQS], Kts[:], Ex[0:NS, T + TS - 1:N:TS],
                              start=True, stop=True).then_inc(a_out, 1)

                pair_block(n + 3, t + 6, 1, outputs)
                pe.wait_ge(a_h, B + 1)
                sample_updates(a_us)
                pe.wait_ge(a_csd, B + 1)
                column_sum(wS, 0, a_mean)
                pe.wait_ge(a_sqs, B + 1)
                column_sum(qs, 2, a_var)

            def gla_head(L, i):
                B = L * HEADS + i
                n = L * LAYER_BLOCKS + i * HEAD_BLOCKS + (BLK_MIX + HEADS * HEAD_BLOCKS)
                t = L * LAYER_TILES + i * HEAD_TILES + (TILE_MIX + GATE_TILES + HEADS * HEAD_TILES)
                pe.wait_ge(b_lr, B * 16 + 16)
                pe.wait_ge(head_done, L * (2 * HEADS) + HEADS + 1 + i)
                for h in range(2):
                    mm = pe.matmul(Q[:, h, 0:HALF], lr2[64:80, :], xg[64:80, h * HALF:(h + 1) * HALF],
                                   start=True, stop=True)
                mm.then_inc(b_z, 1)
                pair_block(n, t, 0)
                block_ready(n + 1)
                value_tiles(t + 2, 1)
                pe.wait_ge(b_fac, B + 1)

                def ring(r):
                    if r >= 4:
                        pe.wait_ge(b_took, B * 10 + (r - 3))
                    return r % 4

                def scores(r):
                    q = ring(r)
                    for c in range(NC):
                        sl = slice(c * C, (c + 1) * C)
                        lhs, rhs = (kT[:, sl], qT[:, sl]) if r == 0 else (seven[:, r - 1, sl], seven[:, r - 1, sl])
                        mm = pe.matmul(Q[:, q, sl], lhs, rhs, start=True, stop=True)
                    mm.then_inc(b_ring, 1)

                for r in range(4):
                    scores(r)

                def more_scores():
                    for r in range(4, 8):
                        scores(r)

                pair_block(n + 2, t + 4, 0, more_scores)
                q = ring(8)
                for c in range(NC):
                    sl = slice(c * C, (c + 1) * C)
                    mm = pe.transpose(Q[:, q, sl], kh[:, sl], ident[:])
                mm.then_inc(b_ring, 1)
                q = ring(9)
                sm = slice(T, N)
                pe.transpose(Q[0:NS, q, P:2 * P], kh[:, sm], ident[:])
                pe.matmul(Q[0:NS, q, 0:NS], kT[:, sm], qT[:, sm], start=True, stop=True)
                for e in range(NLS):
                    lv = seven[:, NL - NLS + e, sm]
                    mm = pe.matmul(Q[0:NS, q, (e + 1) * NS:(e + 2) * NS], lv, lv, start=True, stop=True)
                mm.then_inc(b_ring, 1)

                def update(c):
                    pe.matmul(Q[:, 2 + c % 2, 0:DV], Kw[:, c, :], val[:, c, 0:DV], start=True, stop=True).then_inc(b_u, 1)

                def updates_outputs():
                    pe.wait_ge(b_took, B * 10 + 10)
                    for c in range(NC):
                        if c >= 2:
                            pe.wait_ge(b_c, B * NC + (c - 1))
                        update(c)
                    pe.wait_ge(b_c, B * NC + NC)
                    for v in range(2):
                        vs = slice(v * P, (v + 1) * P)
                        for c in range(NC):
                            sl = slice(c * C, (c + 1) * C)
                            pe.matmul(Q[:, v, sl], val[:, c, vs], wS[:, sl], start=True, stop=c == 0)
                            if c:
                                pe.matmul(Q[:, v, sl], Cst[:, c - 1, vs], qs[:, sl], start=False, stop=True)
                    pe.wait_ge(b_cs, B * 16 + 16)
                    for v in range(2):
                        pe.matmul(Q[:, 2, v * NS:(v + 1) * NS], val[0:NS, NC, v * P:(v + 1) * P], wS[0:NS, sm],
                                  start=True, stop=False, skip_group_check=True)
                        mm = sample_states(2, v, v * NS, lambda s_, v_: CS[:, s_, v_ * P:(v_ + 1) * P])
                    mm.then_inc(b_out, 1)

                pair_block(n + 3, t + 6, 1, updates_outputs)
                pe.wait_ge(b_h, B + 1)
                sample_updates(b_us)
                pe.wait_ge(b_csd, B + 1)
                pe.wait_ge(b_sqs, B + 1)
                column_sum(qs, 0, b_var)

            def lru_pair(L, i, j2):
                pr = L * (KT // 2) + i * 2 + j2
                n = L * LAYER_BLOCKS + i * 6 + (BLK_MIX + 2 * HEADS * HEAD_BLOCKS + 3 * j2)
                t = L * LAYER_TILES + i * 12 + (TILE_MIX + GATE_TILES + 2 * HEADS * HEAD_TILES + 6 * j2)
                if j2 == 0:
                    pe.wait_ge(l_w, L * 64 + i * 32 + 32)

                def gates(j):
                    pe.wait_ge(l_xc, pr * 2 + (j + 1))
                    pe.wait_ge(l_sig, pr * 2 + (j + 1))
                    for w_, b_ in ((wra, 0), (wri, 2)):
                        for h in range(2):
                            mm = pe.matmul(Q[:, b_ + h, 0:HALF], w_[:, 2 * j2 + j, :], xc[:, h * HALF:(h + 1) * HALF],
                                           start=True, stop=True)
                    mm.then_inc(l_ri, 1)

                s0_ = j2 % 2
                pair_block(n, t, s0_)
                gates(0)
                pair_block(n + 1, t + 2, 1 - s0_, lambda: gates(1))
                pair_block(n + 2, t + 4, s0_)

            pe.wait_ge(const_loaded, 16 * CONST_LOADS)
            with pe.Fori(0, DEPTH) as L:
                ffn(L, 0, 0, 0, L * (3 * KT) + KT)
                gate_block(L)
                with pe.Fori(0, HEADS) as i:
                    mlstm_head(L, i)
                with pe.Fori(0, HEADS) as i:
                    gla_head(L, i)
                with pe.Fori(0, KT // 4) as i:
                    lru_pair(L, i, 0)
                    lru_pair(L, i, 1)
                with pe.Fori(0, OUT_BLOCKS // 2) as i:
                    for j in range(2):
                        n = L * LAYER_BLOCKS + i * 2 + (BLK_OUT + j)
                        t = L * LAYER_TILES + i * 4 + (TILE_OUT + 2 * j)
                        block_ready(n)
                        pe.wait_ge(m_ready, L * KT + (KT - 1))
                        for e in range(2):
                            tile(t + e, e, KT, 2 * P, e * P, act=(mh, ml), weights=(wh[:, j], wl[:, j]),
                                 late=lambda: pe.wait_ge(m_ready, L * KT + KT))
                ffn(L, BLK_FFN2, TILE_FFN2, sum(FF_HALVES), L * (3 * KT) + 3 * KT)
            pe.wait_ge(acc_ready, DEPTH * 3 * KT + KT)
            norm_squares().then_inc(norm_sum, 1)

        @block.scalar
        def _(act):
            chain = Chain(act, act_chain, init_done)

            col = 0
            for dst in (ident, ones, neg_p, neg_s, seqm, reset):
                width = dst.shape[1]
                act.dma_start(dst[:], consts[0:dst.shape[0], col:col + width]).then_inc(const_loaded, 16)
                col += width
            act.dma_start(masks[:], level_masks).then_inc(const_loaded, 16)
            act.dma_start(bif[:], b_if).then_inc(const_loaded, 16)
            act.dma_start(m0t[:], m0).then_inc(const_loaded, 16)
            act.wait_ge(init_done, 1)
            act.wait_ge(const_loaded, 16 * CONST_LOADS)

            def ln_1p_exp_neg_abs(dst, src, done):
                chain.link(act.activation(dst, src, ACT.Abs))
                chain.link(act.activation(dst, dst, ACT.Exp, scale=-1.0))
                act.activation(dst, dst, ACT.Ln, bias=one_t[0:dst.shape[0], :]).then_inc(done, 1)

            for l in range(DEPTH):
                ln_1p_exp_neg_abs(c8[:, l * KT:(l + 1) * KT],
                                  V[:, l * V_COLS + V_LAM:l * V_COLS + V_LAM + KT], c8_in)

            act.wait_ge(x_loaded, 16)
            for m in range(KT):
                if m:
                    act.wait_ge(acc_ready, m)
                act.activation(sq[:], x[:, m, :], ACT.Square).then_inc(sq_ready, 1)

            def norm_root(k, tokens_too=False):
                act.wait_ge(norm_sum, k + 1)
                if tokens_too:
                    act.activation(sdT[:], Q[:, 2, 0:NC + 1], ACT.Sqrt, bias=eps_t[:], scale=1.0 / D)
                act.activation(halves(sd[:]), banks(Q[:, 0:2]), ACT.Sqrt, bias=eps_t[:],
                               scale=1.0 / D).then_inc(sd_ready, 1)

            def tile_taken(t):
                act.wait_ge(tile_free, t + 3)

            def squares(t, m):
                tile_taken(t)
                act.activation(sq[:], x[:, m, :], ACT.Square).then_inc(sq_ready, 1)

            def ffn(L, first_tile, norm):
                t = L * LAYER_TILES + first_tile
                norm_root(norm)
                for half, tiles in enumerate(FF_HALVES):
                    with act.Fori(0, tiles // 2) as i:
                        for j in range(2):
                            tile_taken(i * 4 + (t + 2 * j))
                            act.activation(sg[:], gs[:], ACT.Silu).then_inc(silu_done, 1)
                    t = t + 2 * tiles
                    if half == 1:
                        with act.Fori(0, KT // 2) as i:
                            for j in range(2):
                                squares(i * 2 + (t + j), i * 2 + j)
                    t = t + KT

            def gate_tiles(t):
                for v in range(2):
                    tile_taken(t + v)
                    act.activation(Gm[:, v, :], tg[:], ACT.Sigmoid).then_inc(gate_act, 1)
                yield
                for v in range(2):
                    tile_taken(t + 2 + v)
                    act.activation(tg[:], tg[:], ACT.Sigmoid).then_inc(gate_act, 1)

            def head_root(bank, done):
                act.activation(halves(seven[:, 2, :]), banks(Q[:, bank:bank + 2]), ACT.Sqrt, bias=eps_t[:],
                               scale=1.0 / DV).then_inc(done, 1)

            def mlstm_head(L, i):
                B = L * HEADS + i
                t = L * LAYER_TILES + i * HEAD_TILES + (TILE_MIX + GATE_TILES)
                stored = L * (16 * STORES) + i * 48 + 32
                act.wait_ge(head_done, L * (2 * HEADS) + i + 1)
                act.wait_ge(rows_stored, L * 16 + 16)
                act.dma_start(RB.rearrange("p a b -> p (a b)"),
                              spread(rows_dram[ds(i, 1), :], 0, P)).then_inc(a_rows, 16)
                act.wait_ge(a_rows, B * 16 + 16)
                act.activation(SI, RB[:, 1, :], ACT.Exp)
                act.activation(EM, RB[:, 2, :], ACT.Exp).then_inc(a_si, 1)
                act.wait_ge(state_stored, stored)
                act.dma_start(CS[:], c0[L, i]).then_inc(a_cs, 16)
                act.dma_start(nS[:, 0, :], n0[L, i]).then_inc(a_cs, 16)
                act.wait_ge(a_exin, B + 1)
                for c in range(NC):
                    sl = slice(c * C, (c + 1) * C)
                    act.activation(Ex[:, sl], Ex[:, sl], ACT.Exp, bias=cols[:, c:c + 1])
                act.activation(Ex[0:NS, T:N], Ex[0:NS, T:N], ACT.Exp, bias=cols[0:NS, NC:NC + 1]).then_inc(a_ex, 1)
                gates = gate_tiles(t + 4)
                next(gates)
                act.wait_ge(a_c, B * NC + NC)
                act.dma_start(o_pc[L, i], Cst[:, NC - 1, 0:DV + 1]).then_inc(state_stored, 16)
                next(gates, None)
                act.wait_ge(a_csd, B + 1)
                act.dma_start(o_sc[L, i], CS[:]).then_inc(state_stored, 16)
                act.dma_start(o_sn[L, i], nS[:, 1, :]).then_inc(state_stored, 16)
                act.wait_ge(a_hc, B + 1)
                act.activation(seven[:, 0:2, :], Hh[:], ACT.Square).then_inc(a_sq, 1)
                act.wait_ge(a_var, B + 1)
                head_root(2, a_sd)

            def gla_head(L, i):
                B = L * HEADS + i
                t = L * LAYER_TILES + i * HEAD_TILES + (TILE_MIX + GATE_TILES + HEADS * HEAD_TILES)
                stored = L * (16 * STORES) + i * 32 + (32 + 48 * HEADS)
                act.wait_ge(head_done, L * (2 * HEADS) + i + (HEADS + 1))
                act.dma_start(lr2[64:80, :], w_lr2[L, i]).then_inc(b_lr, 16)
                chain.restart()
                act.wait_ge(b_zin, B + 1)
                ln_1p_exp_neg_abs(seven[:, 1, :], seven[:, 0, :], b_ln)
                act.wait_ge(state_stored, stored)
                act.dma_start(CS[:], s0[L, i]).then_inc(b_cs, 16)
                act.wait_ge(b_diff, B + 1)
                inv = 1.0 / 16.0
                act.activation(seven[:, 0:NL - NLS, 0:T], seven[:, 0:NL - NLS, 0:T], ACT.Exp, scale=inv)
                act.activation(seven[:, NL - NLS:NL, :], seven[:, NL - NLS:NL, :], ACT.Exp, scale=inv)
                act.activation(eb[:], bc[:], ACT.Exp, scale=inv)
                act.activation(kh[:], kh[:], ACT.Exp, scale=inv).then_inc(b_exp, 1)
                gates = gate_tiles(t + 4)
                next(gates)
                next(gates, None)
                act.wait_ge(b_c, B * NC + NC)
                act.dma_start(o_ps[L, i], Cst[:, NC - 1, 0:DV]).then_inc(state_stored, 16)
                act.wait_ge(b_h, B + 1)
                act.activation(seven[:, 0:2, :], Hh[:], ACT.Square).then_inc(b_sq, 1)
                act.wait_ge(b_csd, B + 1)
                act.dma_start(o_ss[L, i], CS[:]).then_inc(state_stored, 16)
                act.wait_ge(b_var, B + 1)
                head_root(0, b_sd)

            def lru_pair(L, i, j2):
                pr = L * (KT // 2) + i * 2 + j2
                t = L * LAYER_TILES + i * 12 + (TILE_MIX + GATE_TILES + 2 * HEADS * HEAD_TILES + 6 * j2)

                def gates(j):
                    k = pr * 2 + j
                    g = L * V_COLS + i * 4 + (2 * j2 + j)
                    act.wait_ge(l_ri, k + 1)
                    act.activation(halves(rr[:]), banks(Q[:, 0:2]), ACT.Sigmoid, bias=V[:, ds(g + V_BA, 1)])
                    act.activation(halves(ii[:]), banks(Q[:, 2:4]), ACT.Sigmoid,
                                   bias=V[:, ds(g + V_BI, 1)]).then_inc(l_sig, 1)
                    act.wait_ge(l_sig, k + 2)
                    c = L * KT + i * 4 + (2 * j2 + j)
                    act.activation(aa[:], rr[:], ACT.Exp, scale=c8[:, ds(c, 1)])
                    act.activation(tt[:], rr[:], ACT.Tanh, scale=nc8[:, ds(c, 1)]).then_inc(l_at, 1)
                    act.wait_ge(l_min, k + 1)
                    act.activation(tt[:], tt[:], ACT.Sqrt).then_inc(l_mult, 1)

                def gelu(v):
                    tile_taken(t + 2 + v)
                    act.activation(lyg[:, v, :], lyg[:, v, :], ACT.Gelu_apprx_tanh).then_inc(l_act, 1)

                gates(0)
                gelu(0)
                gates(1)
                gelu(1)
                for v in range(2):
                    tile_taken(t + 4 + v)
                    act.activation(tt[:], tt[:], ACT.Sigmoid).then_inc(l_act, 1)

            with act.Fori(0, DEPTH) as L:
                ffn(L, 0, L * 3)
                norm_root(L * 3 + 1, tokens_too=True)
                chain.restart()
                act.wait_ge(gate_in, L + 1)
                ln_1p_exp_neg_abs(merged[0:HEADS, 6, :], merged[0:HEADS, 5, :], gate_ln)
                act.wait_ge(rows_ready, L + 1)
                act.dma_start(rows_dram, merged[0:HEADS, 0:4, :].rearrange("h a b -> h (a b)")).then_inc(rows_stored, 16)
                act.dma_start(o_pm[L], m_out[:, 0:1]).then_inc(state_stored, 16)
                act.dma_start(o_sm[L], m_out[:, 1:]).then_inc(state_stored, 16)
                with act.Fori(0, HEADS) as i:
                    mlstm_head(L, i)
                with act.Fori(0, HEADS) as i:
                    gla_head(L, i)
                act.wait_ge(head_done, L * (2 * HEADS) + (2 * HEADS + 1))
                act.wait_ge(state_stored, L * (16 * STORES) + 16 * (STORES - 4))
                act.dma_start(h0t[:], h0[L]).then_inc(l_vec, 16)
                act.dma_start(cv0[:], conv0[L]).then_inc(l_vec, 16)
                with act.Fori(0, KT // 4) as i:
                    act.dma_start(wra[:], w_ra[L, i]).then_inc(l_w, 16)
                    act.dma_start(wri[:], w_ri[L, i]).then_inc(l_w, 16)
                    lru_pair(L, i, 0)
                    lru_pair(L, i, 1)
                act.wait_ge(lru_done, L * (KT // 2) + KT // 2 + 1)
                for dst, src in ((o_ph[L], ph), (o_sh[L], sh), (o_pconv[L], pcv), (o_sconv[L], scv)):
                    act.dma_start(dst, src[:]).then_inc(state_stored, 16)
                with act.Fori(0, KT // 2) as i:
                    for j in range(2):
                        squares(L * LAYER_TILES + i * 2 + (TILE_OUT + j), i * 2 + j)
                ffn(L, TILE_FFN2, L * 3 + 2)
            chain.end()
            norm_root(3 * DEPTH)

        @block.vector
        def _(dve):
            chain = Chain(dve, dve_chain, init_done)
            link = chain.link
            tt_, ts_, stt = dve.tensor_tensor, dve.tensor_scalar, dve.scalar_tensor_tensor
            rs2 = halves(rstd[:])

            def tile_ready(t):
                dve.wait_ge(tile_done, t + 3)

            def take(t, slot, dst, scale=None):
                tile_ready(t)
                if scale is None:
                    ins = tt_(halves(dst), banks(pair[slot]), rs2, ALU.mult)
                else:
                    ins = stt(halves(dst), banks(pair[slot]), scale, rs2, ALU.mult, ALU.mult)
                ins.then_inc(tile_free, 1)
                dve.wait_ge(tile_free, t + 3)

            def prepare(m, g_col, n_sq):
                link(ts_(xg[:], x[:, m, :], V[:, ds(g_col, 1)], None, ALU.mult))
                link(dve.tensor_copy(xh[:, m, :], xg[:]))
                tt_(xl[:, m, :], xg[:], xh[:, m, :].bitcast(F32), ALU.subtract)
                dve.wait_ge(sq_ready, n_sq + 1)
                tt_(acc[:], acc[:], sq[:], ALU.add).then_inc(acc_ready, 1)
                dve.wait_ge(acc_ready, n_sq + 1)

            def residual(t, slot, m, scale):
                tile_ready(t)
                stt(halves(x[:, m, :]), banks(pair[slot]), scale, halves(x[:, m, :]),
                    ALU.mult, ALU.add).then_inc(tile_free, 1)
                dve.wait_ge(tile_free, t + 3)

            def clear_acc():
                chain.restart()
                link(dve.memset(acc[:], 0.0))

            def reciprocal_norm(k):
                dve.wait_ge(sd_ready, k + 1)
                chain.restart()
                link(dve.reciprocal(rstd[:], sd[:]))

            def ffn(L, first_tile, h_base, norm, g_col):
                t = L * LAYER_TILES + first_tile
                hd = L * (2 * sum(FF_HALVES)) + h_base
                reciprocal_norm(norm)
                for half, tiles in enumerate(FF_HALVES):
                    with dve.Fori(0, tiles // 2) as i:
                        chain.restart()
                        for j in range(2):
                            tj = i * 4 + (t + 2 * j)
                            take(tj, 0, gs[:])
                            take(tj + 1, 1, us[:])
                            dve.wait_ge(silu_done, hd + i * 2 + (j + 1))
                            link(tt_(hp[:], sg[:], us[:], ALU.mult))
                            hi = hh[:, i * 2 + j, :]
                            link(dve.tensor_copy(hi, hp[:]))
                            tt_(hl[:, i * 2 + j, :], hp[:], hi.bitcast(F32), ALU.subtract).then_inc(h_done, 1)
                            dve.wait_ge(h_done, hd + i * 2 + (j + 1))
                    t, hd = t + 2 * tiles, hd + tiles
                    if half == 1:
                        clear_acc()
                    with dve.Fori(0, KT // 2) as i:
                        chain.restart()
                        for j in range(2):
                            residual(i * 2 + (t + j), j, i * 2 + j, 0.5)
                            if half == 1:
                                prepare(i * 2 + j, g_col + i * 2 + j, norm * KT + i * 2 + (KT + j))
                    t = t + KT

            dve.wait_ge(const_loaded, 16 * CONST_LOADS)
            dve.wait_ge(c8_in, DEPTH)
            for l in range(DEPTH):
                s_ = slice(l * KT, (l + 1) * KT)
                lam = V[:, l * V_COLS + V_LAM:l * V_COLS + V_LAM + KT]
                link(ts_(t8[:, 0:KT], lam, -1.0, 0.0, ALU.mult, ALU.max))
                link(tt_(t8[:, 0:KT], t8[:, 0:KT], c8[:, s_], ALU.add))
                link(ts_(c8[:, s_], t8[:, 0:KT], -8.0, None, ALU.mult))
                link(ts_(nc8[:, s_], t8[:, 0:KT], 8.0, None, ALU.mult))
            dve.memset(t8[:], 0.0).then_inc(tile_free, 2)
            dve.wait_ge(tile_free, 2)
            dve.memset(t8[:], 0.0).then_inc(head_done, 1)
            dve.wait_ge(head_done, 1)
            dve.memset(t8[:], 0.0).then_inc(l_sig, 1)
            dve.wait_ge(l_sig, 1)
            dve.memset(t8[:], 0.0).then_inc(lru_done, 1)
            dve.wait_ge(lru_done, 1)
            dve.wait_ge(x_loaded, 16)
            clear_acc()
            for m in range(KT):
                prepare(m, V_FIRST + m, m)

            def gate_rows(L):
                R = [merged[0:HEADS, r, :] for r in range(KT)]
                tile_ready(L * LAYER_TILES + (TILE_MIX + 1))
                g = banks(pair[0])
                link(tt_(halves(R[4]), g[0:HEADS], rs2[0:HEADS], ALU.mult))
                link(tt_(halves(R[5]), g[32:32 + HEADS], rs2[32:32 + HEADS], ALU.mult))
                tt_(halves(glr), g[64:80], rs2[64:80], ALU.mult).then_inc(tile_free, GATE_TILES)
                link(ts_(R[4], R[4], bif[:, ds(L, 1), 0], None, ALU.add))
                ts_(R[5], R[5], bif[:, ds(L, 1), 1], None, ALU.add).then_inc(gate_in, 1)
                dve.wait_ge(gate_ln, L + 1)
                link(stt(R[7], R[5], 0.0, R[6], ALU.min, ALU.subtract))
                link(dve.tensor_tensor_scan(R[5], reset[0:HEADS, :], R[7], 0.0, ALU.mult, ALU.add))
                link(tt_(R[3], R[4], R[5], ALU.subtract))
                m0_ = m0t[:, ds(L, 1), :].rearrange("p a s -> p (a s)")
                link(tt_(t8[0:HEADS, :], R[7][:, T:N:TS], m0_, ALU.add))
                link(dve.tensor_copy(R[6], R[7]))
                link(dve.memset(R[6][:, T:N:TS], NEG))
                link(dve.tensor_copy(R[0], R[4]))
                link(tt_(R[0][:, T:N:TS], R[4][:, T:N:TS], t8[0:HEADS, :], ALU.max))
                link(dve.tensor_tensor_scan(R[7], R[6], R[0], 0.0, ALU.add, ALU.max))
                link(ts_(R[2], R[7], -1.0, None, ALU.mult))
                link(tt_(R[0], R[5], R[7], ALU.subtract))
                link(dve.tensor_copy(R[1][:, 0:C], R[0][:, 0:C]))
                for c in range(1, NC):
                    link(ts_(R[1][:, c * C:(c + 1) * C], R[0][:, c * C:(c + 1) * C], R[7][:, c * C - 1:c * C],
                             None, ALU.add))
                sv = [r[:, T:N].rearrange("p (s t) -> p s t", t=TS) for r in R]
                link(tt_(sv[1], sv[0], spread(m0_.unsqueeze(2), 2, TS), ALU.add))
                link(dve.tensor_copy(m_out[:, 0:1], R[7][:, T - 1:T]))
                dve.tensor_copy(m_out[:, 1:], R[7][:, T + TS - 1:N:TS]).then_inc(rows_ready, 1)

            def take_values(t):
                tile_ready(t)
                tt_(val[:, 0:NC, 0:DV], pair[0][:].rearrange("p a (b v) -> p (a b) v", b=2),
                    spread(rstdT[:, 0:NC].unsqueeze(2), 2, DV), ALU.mult).then_inc(tile_free, 1)
                tile_ready(t + 1)
                ts_(val[0:NS, NC, 0:DV], pair[1][C - NS:C, 0, 0:DV], rstdT[C - NS:C, NC:NC + 1], None,
                    ALU.mult).then_inc(tile_free, 1)
                dve.wait_ge(tile_free, t + 4)

            def take_gate(L, i, t, slot, v, acts, kind, g_col):
                take(t, slot, tg[:])
                dve.wait_ge(gate_act, acts + 1)
                if kind == "silu":
                    link(tt_(Gm[:, v, :], Gm[:, v, :], tg[:], ALU.mult))
                if kind == "branch":
                    link(stt(Gm[:, v, :], Gm[:, v, :], V[:, ds(g_col, 1)], tg[:], ALU.mult, ALU.mult))

            def states(c_, width, dec, b_of, up, done, base):
                dve.wait_ge(up, base + (c_ + 1))
                src = Q[:, b_of(c_), 0:width]
                if c_ == 0:
                    ins = dve.tensor_copy(Cst[:, 0, 0:width], src)
                else:
                    ins = stt(Cst[:, c_, 0:width], Cst[:, c_ - 1, 0:width], dec(c_), src, ALU.mult, ALU.add)
                ins.then_inc(done, 1)
                dve.wait_ge(done, base + (c_ + 1))

            def sample_states(decay):
                for s_ in range(SEQS):
                    k = T + s_ * TS + TS - 1
                    ins = stt(CS[:, s_, :], CS[:, s_, :], decay[:, k:k + 1],
                              Q[:, s_ // 2, s_ % 2 * DV:(s_ % 2 + 1) * DV], ALU.mult, ALU.add)
                return ins

            def finish_head(L, i, sd_sem, sd_at, first, number):
                dve.wait_ge(sd_sem, sd_at)
                link(dve.reciprocal(seven[:, 3, :], seven[:, 2, :]))
                r = spread(seven[:, 3, :].unsqueeze(1), 1, 2)
                link(tt_(Hh[:], Hh[:], Gm[:], ALU.mult))
                mo_ = merged[:, ds(i * 2, 2), :]
                if first:
                    ins = tt_(mo_, Hh[:], r, ALU.mult)
                else:
                    link(tt_(Hh[:], Hh[:], r, ALU.mult))
                    ins = tt_(mo_, mo_, Hh[:], ALU.add)
                ins.then_inc(head_done, 1)
                dve.wait_ge(head_done, number + 2)

            def mlstm_head(L, i):
                B = L * HEADS + i
                t = L * LAYER_TILES + i * HEAD_TILES + (TILE_MIX + GATE_TILES)
                acts = L * (8 * HEADS) + i * 4
                gcol = L * V_COLS + i * 2 + V_GML
                chain.restart()
                take(t, 0, qT[:])
                take(t + 1, 1, kT[:], DK ** -0.5)
                dve.wait_ge(a_si, B + 1)
                link(tt_(qs[:], qT[:], SI, ALU.mult))
                take_values(t + 2)
                link(tt_(Ex[:, 0:T].rearrange("p (c t) -> p c t", c=NC),
                         RB[:, 0, 0:T].rearrange("p (c t) -> p c t", c=NC),
                         spread(neg_p[:].unsqueeze(1), 1, NC), ALU.add))
                link(tt_(Ex[0:NS, T:N], RB[0:NS, 0, T:N], neg_s[:], ALU.add))
                dve.wait_ge(a_cs, B * 32 + 32)
                link(dve.tensor_copy(nB[:], spread(nS[:, 0, :].unsqueeze(2), 2, P)))
                dve.wait_ge(a_scores, B + 1)
                link(dve.tensor_copy(cols[0:NS, NC:NC + 1], Q[0:NS, 2, 200 + NC:201 + NC]))
                dve.tensor_copy(cols[:, 0:NC], Q[:, 2, 200:200 + NC]).then_inc(a_exin, 1)
                dve.wait_ge(a_ex, B + 1)
                exv = Ex[:, 0:T].rearrange("p (c t) -> p c t", c=NC)
                link(tt_(wS[:, 0:T], Ex[:, 0:T], Q[:, 0, :], ALU.mult))
                link(tt_(wS[0:NS, T:N], Ex[0:NS, T:N], Q[0:NS, 2, 0:NS], ALU.mult))
                link(tt_(Kw[:], Q[:, 1, :].rearrange("p (c t) -> p c t", c=NC),
                         spread(exv[:, :, C - 1:C], 2, P), ALU.mult))
                link(dve.tensor_copy(Kts[:], Q[0:NS, 2, NS:NS + P]))
                tt_(Kws[:], spread(Kts[:].unsqueeze(1), 1, SEQS),
                    spread(Ex[0:NS, T + TS - 1:N:TS].unsqueeze(2), 2, P), ALU.mult).then_inc(a_kw, 1)

                def state(c_):
                    states(c_, DV + P, lambda c: SI[:, c * C + C - 1:(c + 1) * C], lambda c: 3 - c % 2,
                           a_u, a_c, B * NC)

                take_gate(L, i, t + 4, 0, 0, acts, "sigmoid", None)
                state(0)
                state(1)
                take_gate(L, i, t + 5, 1, 1, acts + 1, "sigmoid", None)
                state(2)
                state(3)
                take_gate(L, i, t + 6, 0, 0, acts + 2, "branch", gcol)
                dve.wait_ge(a_out, B + 1)
                for sl, den in ((slice(0, T), Q[:, 2, :]), (slice(T, N), Q[:, 3, 2 * NS:3 * NS])):
                    link(stt(tg[:, sl], den, -1.0, EM[:, sl], ALU.mult, ALU.max))
                    link(tt_(tg[:, sl], tg[:, sl], den, ALU.max))
                link(dve.reciprocal(tg[:], tg[:]))
                link(tt_(Hh[:, :, 0:T], Q[:, 0:2, :], spread(tg[:, 0:T].unsqueeze(1), 1, 2), ALU.mult))
                link(tt_(Hh[:, :, T:N], Q[:, 3, 0:2 * NS].rearrange("p (v t) -> p v t", v=2),
                         spread(tg[:, T:N].unsqueeze(1), 1, 2), ALU.mult))
                link(tt_(nS[:, 1, :], nS[:, 0, :], SI[:, T + TS - 1:N:TS], ALU.mult))
                link(tt_(nS[:, 1, :], nS[:, 1, :], Q[:, 3, 3 * NS:3 * NS + SEQS], ALU.add))
                tt_(wS[:], Hh[:, 0, :], Hh[:, 1, :], ALU.add).then_inc(a_h, 1)
                take_gate(L, i, t + 7, 1, 1, acts + 3, "branch", gcol + 1)
                dve.wait_ge(a_us, B + 1)
                sample_states(SI).then_inc(a_csd, 1)
                dve.wait_ge(a_mean, B + 1)
                for v in range(2):
                    ins = stt(halves(Hh[:, v, :]), banks(Q[:, 0:2]), -1.0 / DV, halves(Hh[:, v, :]), ALU.mult, ALU.add)
                ins.then_inc(a_hc, 1)
                dve.wait_ge(a_sq, B + 1)
                tt_(qs[:], seven[:, 0, :], seven[:, 1, :], ALU.add).then_inc(a_sqs, 1)
                finish_head(L, i, a_sd, B + 1, True, L * (2 * HEADS) + i)

            def gla_head(L, i):
                B = L * HEADS + i
                t = L * LAYER_TILES + i * HEAD_TILES + (TILE_MIX + GATE_TILES + HEADS * HEAD_TILES)
                acts = L * (8 * HEADS) + i * 4 + 4 * HEADS
                gcol = L * V_COLS + i * 2 + V_GGLA
                chain.restart()
                dve.wait_ge(b_z, B + 1)
                z, l_, la = seven[:, 0, :], seven[:, 1, :], seven[:, 2, :]
                ts_(halves(z), banks(Q[:, 0:2]), V[:, ds(L * V_COLS + i + V_BGLA, 1)], None,
                    ALU.add).then_inc(b_zin, 1)
                dve.wait_ge(b_ln, B + 1)
                link(stt(la, z, 0.0, l_, ALU.min, ALU.subtract))
                link(dve.tensor_tensor_scan(bc[:], reset[:], la, 0.0, ALU.mult, ALU.add))
                for l in range(NL):
                    h_ = LEVELS[l]
                    m_ = N if l >= NL - NLS else T
                    bv = bc[:, 0:m_].rearrange("p (n a h) -> p n a h", a=2, h=h_)
                    ev = seven[:, l, 0:m_].rearrange("p (n a h) -> p n a h", a=2, h=h_)
                    mid = spread(bv[:, :, 0, h_ - 1:h_], 2, h_)
                    tt_(ev[:, :, 1, :], bv[:, :, 1, :], mid, ALU.subtract)
                    ins = tt_(ev[:, :, 0, :], mid, bv[:, :, 0, :], ALU.subtract)
                link(ins)
                bp = bc[:, 0:T].rearrange("p (c t) -> p c t", c=NC)
                bs = bc[:, T:N].rearrange("p (c t) -> p c t", c=SEQS)
                tt_(kh[:, 0:T].rearrange("p (c t) -> p c t", c=NC), spread(bp[:, :, C - 1:C], 2, C), bp, ALU.subtract)
                tt_(kh[:, T:N].rearrange("p (c t) -> p c t", c=SEQS), spread(bs[:, :, TS - 1:TS], 2, TS), bs,
                    ALU.subtract).then_inc(b_diff, 1)
                take(t, 0, qT[:], DK ** -0.5)
                take(t + 1, 1, kT[:])
                dve.wait_ge(b_exp, B + 1)
                for l in range(NL):
                    h_ = LEVELS[l]
                    m_ = N if l >= NL - NLS else T
                    ev = seven[:, l, 0:m_].rearrange("p (n a h) -> p n a h", a=2, h=h_)
                    for a, src in ((1, qT), (0, kT)):
                        sv = src[:, 0:m_].rearrange("p (n a h) -> p n a h", a=2, h=h_)
                        tt_(ev[:, :, a, :], ev[:, :, a, :], sv[:, :, a, :], ALU.mult)
                tt_(qs[:], qT[:], eb[:], ALU.mult)
                link(tt_(kh[:], kh[:], kT[:], ALU.mult))
                take_values(t + 2)
                dve.memset(t8[:], 0.0).then_inc(b_fac, 1)

                def took():
                    return B * 10

                def ring(r):
                    dve.wait_ge(b_ring, B * 10 + (r + 1))

                def level(r):
                    ring(r)
                    av = wS[:, 0:T].rearrange("p (c t) -> p c t", c=NC)
                    src = Q[:, r % 4, :].rearrange("p (c t) -> p c t", c=NC)
                    if r == 0:
                        ins = tt_(av, src, spread(ident[:].unsqueeze(1), 1, NC), ALU.mult)
                    else:
                        chain.hold()
                        ins = dve.copy_predicated(av, spread(masks[:, r - 1, :].unsqueeze(1), 1, NC), src)
                    ins.then_inc(b_took, 1)
                    dve.wait_ge(b_took, B * 10 + (r + 1))

                for r in range(4):
                    level(r)
                take_gate(L, i, t + 4, 0, 0, acts, "silu", None)
                for r in range(4, 8):
                    level(r)
                take_gate(L, i, t + 5, 1, 1, acts + 1, "silu", None)
                ring(8)
                dve.tensor_copy(Kw[:], Q[:, 0, :].rearrange("p (c t) -> p c t", c=NC)).then_inc(b_took, 1)
                ring(9)
                As = wS[0:NS, T:N]
                link(tt_(As, Q[0:NS, 1, 0:NS], ident[0:NS, 0:NS], ALU.mult))
                for e in range(NLS):
                    link(dve.copy_predicated(As, masks[0:NS, NL - NLS + e, 0:NS], Q[0:NS, 1, (e + 1) * NS:(e + 2) * NS]))
                tt_(Kws[:], spread(Q[0:NS, 1, P:2 * P].unsqueeze(1), 1, SEQS),
                    spread(seqm[:].unsqueeze(2), 2, P), ALU.mult).then_inc(b_took, 1)
                take_gate(L, i, t + 6, 0, 0, acts + 2, "branch", gcol)
                for c in range(NC):
                    states(c, DV, lambda c_: eb[:, c_ * C + C - 1:(c_ + 1) * C], lambda c_: 2 + c_ % 2, b_u, b_c, B * NC)
                dve.wait_ge(b_out, B + 1)
                dve.tensor_copy(Hh[:, :, 0:T], Q[:, 0:2, :])
                dve.tensor_copy(Hh[:, :, T:N], Q[:, 2, 0:2 * NS].rearrange("p (v t) -> p v t", v=2)).then_inc(b_h, 1)
                take_gate(L, i, t + 7, 1, 1, acts + 3, "branch", gcol + 1)
                dve.wait_ge(b_us, B + 1)
                sample_states(eb).then_inc(b_csd, 1)
                dve.wait_ge(b_sq, B + 1)
                tt_(qs[:], seven[:, 0, :], seven[:, 1, :], ALU.add).then_inc(b_sqs, 1)
                finish_head(L, i, b_sd, B + 1, False, L * (2 * HEADS) + HEADS + i)

            def lru_pair(L, i, j2):
                pr = L * (KT // 2) + i * 2 + j2
                t = L * LAYER_TILES + i * 12 + (TILE_MIX + GATE_TILES + 2 * HEADS * HEAD_TILES + 6 * j2)
                chain.restart()

                def at(j):
                    return i * 4 + (2 * j2 + j)

                def take_x(j):
                    tile_ready(t + j)
                    tt_(lxp[:, j, 3:3 + HALF], pair[j][:, 0, 0:HALF], rstd[:, 0:HALF], ALU.mult)
                    tt_(lxp[:, j, 3 + HALF:3 + T], pair[j][:, 1, 0:T - HALF], rstd[:, HALF:T], ALU.mult)
                    dve.tensor_copy(lxs[:, j, :, 0:3], cv0[:, at(j), :, :])
                    tt_(lxs[:, j, :, 3:3 + TS],
                        pair[j][:, 1, T - HALF:HALF].rearrange("p (s t) -> p s t", t=TS),
                        rstd[:, T:N].rearrange("p (s t) -> p s t", t=TS), ALU.mult).then_inc(tile_free, 1)
                    dve.wait_ge(tile_free, t + (j + 3))

                def conv(j):
                    col = L * V_COLS + i * 4 + (2 * j2 + j)
                    xs = xc[:, T:N].rearrange("p (s t) -> p s t", t=TS)
                    w = [V[:, ds(col + (V_CONV + KT * a), 1)] for a in range(4)]
                    b = V[:, ds(col + V_BCONV, 1)]
                    ts_(xc[:, 0:T], lxp[:, j, 0:T], w[0], b, ALU.mult, ALU.add)
                    link(ts_(xs, lxs[:, j, :, 0:TS], w[0], b, ALU.mult, ALU.add))
                    for a in range(1, 4):
                        stt(xc[:, 0:T], lxp[:, j, a:a + T], w[a], xc[:, 0:T], ALU.mult, ALU.add)
                        ins = stt(xs, lxs[:, j, :, a:a + TS], w[a], xs, ALU.mult, ALU.add)
                        if a < 3:
                            link(ins)
                    ins.then_inc(l_xc, 1)
                    dve.tensor_copy(pcv[:, at(j), :], lxp[:, j, T:T + 3])
                    dve.tensor_copy(scv[:, at(j), :, :], lxs[:, j, :, TS:TS + 3])

                def recur(j):
                    k = pr * 2 + j
                    dve.wait_ge(l_at, k + 1)
                    link(tt_(hseq[:, j, :], aa[:], aa[:], ALU.mult))
                    stt(tt[:], hseq[:, j, :], 1.0, tt[:], ALU.add, ALU.mult).then_inc(l_min, 1)
                    link(tt_(ii[:], ii[:], xc[:], ALU.mult))
                    dve.wait_ge(l_mult, k + 1)
                    link(dve.memset(tt[:, 0:1], 1.0))
                    link(tt_(ii[:], ii[:], tt[:], ALU.mult))
                    starts = slice(T, N, TS)
                    link(tt_(t8[:], aa[:, starts], h0t[:, at(j), :], ALU.mult))
                    link(tt_(ii[:, starts], ii[:, starts], t8[:], ALU.add))
                    link(dve.memset(aa[:, starts], 0.0))
                    link(dve.tensor_tensor_scan(hseq[:, j, :], aa[:], ii[:], 0.0, ALU.mult, ALU.add))
                    dve.tensor_copy(ph[:, ds(at(j), 1)], hseq[:, j, T - 1:T])
                    link(dve.tensor_copy(sh[:, at(j), :], hseq[:, j, T + TS - 1:N:TS]))

                def take_y(v):
                    take(t + 2 + v, v, lyg[:, v, :])

                take_x(0)
                conv(0)
                take_x(1)
                recur(0)
                conv(1)
                take_y(0)
                recur(1)
                take_y(1)
                for v in range(2):
                    take(t + 4 + v, v, tt[:])
                    dve.wait_ge(l_act, pr * 4 + (3 + v))
                    link(tt_(tt[:], tt[:], lyg[:, v, :], ALU.mult))
                    link(tt_(tt[:], tt[:], hseq[:, v, :], ALU.mult))
                    link(tt_(tt[:], tt[:], merged[:, at(v), :], ALU.add))
                    link(dve.tensor_copy(mh[:, at(v), :], tt[:]))
                    tt_(ml[:, at(v), :], tt[:], mh[:, at(v), :].bitcast(F32), ALU.subtract).then_inc(m_ready, 1)
                    dve.wait_ge(m_ready, pr * 2 + (v + 1))
                dve.memset(t8[:], 0.0).then_inc(lru_done, 1)
                dve.wait_ge(lru_done, pr + 2)

            with dve.Fori(0, DEPTH) as L:
                ffn(L, 0, 0, L * 3, L * V_COLS + V_MIX)
                reciprocal_norm(L * 3 + 1)
                link(dve.reciprocal(rstdT[:], sdT[:]))
                gate_rows(L)
                dve.wait_ge(rows_ready, L + 1)
                chain.restart()
                link(dve.memset(val[:, :, DV:DV + P], 1.0))
                with dve.Fori(0, HEADS) as i:
                    mlstm_head(L, i)
                with dve.Fori(0, HEADS) as i:
                    gla_head(L, i)
                chain.restart()
                dve.wait_ge(l_vec, L * 32 + 32)
                link(dve.memset(lxp[:, :, 0:3], 0.0))
                with dve.Fori(0, KT // 4) as i:
                    lru_pair(L, i, 0)
                    lru_pair(L, i, 1)
                clear_acc()
                with dve.Fori(0, KT // 2) as i:
                    chain.restart()
                    for j in range(2):
                        residual(L * LAYER_TILES + i * 2 + (TILE_OUT + j), j, i * 2 + j, 1.0)
                        prepare(i * 2 + j, L * V_COLS + i * 2 + (V_FFN2 + j), L * (3 * KT) + i * 2 + (2 * KT + j))
                dve.wait_ge(state_stored, L * (16 * STORES) + 16 * STORES)
                ffn(L, TILE_FFN2, sum(FF_HALVES), L * 3 + 2, L * V_COLS + V_NEXT)
            reciprocal_norm(3 * DEPTH)
            chain.end()
            for m in range(KT):
                g = (DEPTH - 1) * V_COLS + V_NEXT + m
                stt(x[:, m, :], x[:, m, :], V[:, g:g + 1], rstd[:], ALU.mult, ALU.mult).then_inc(y_ready, 1)


def _layout(inputs):
    import numpy as np

    a = {k: np.asarray(v) for k, v in inputs.items()}
    f = np.float32
    out = {}
    xs = np.concatenate([a["x_prompt"][0], a["x_sample"].reshape(NS, D)])
    out["x_T"] = xs.T.reshape(KT, P, N).transpose(1, 0, 2)

    def up(w):
        w = w.reshape(DEPTH, KT, P, 2, FF // P, P)
        return w.transpose(0, 4, 2, 1, 3, 5).reshape(DEPTH, FF // P, P, 2 * D)

    def down(w):
        w = w.reshape(DEPTH, FF // P, P, KT, P).transpose(0, 3, 2, 1, 4)
        b = np.zeros((DEPTH, 2 * KT, P, FF_HALVES[0] * P), f)
        first = 0
        for h, n in enumerate(FF_HALVES):
            b[:, h * KT:(h + 1) * KT, :, 0:n * P] = w[:, :, :, first:first + n].reshape(DEPTH, KT, P, n * P)
            first += n
        return b

    def blocks(w):
        n = w.shape[2] // (2 * P)
        return w.reshape(DEPTH, KT, P, n, 2 * P).transpose(0, 3, 2, 1, 4).reshape(DEPTH, n, P, 2 * D)

    out["w_up1"], out["w_down1"] = up(a["w_ffn1_in"]), down(a["w_ffn1_out"])
    out["w_up2"], out["w_down2"] = up(a["w_ffn2_in"]), down(a["w_ffn2_out"])
    qk, g8, r16 = HEADS * DK, 2 * HEADS, a["w_gla_lr2"].shape[1]
    sizes = [qk, qk, D, D, g8, qk, qk, D, D, r16, D, D, 3 * D]
    mq, mk, mv, mo, mif, gq, gk, gv, gg, glr_, lx, ly, mg = np.split(a["w_in"], np.cumsum(sizes)[:-1], axis=2)
    order = []
    for q, k, v, o, br in ((mq, mk, mv, mo, 0), (gq, gk, gv, gg, 1)):
        for h in range(HEADS):
            c1, c2 = slice(h * DK, (h + 1) * DK), slice(h * DV, (h + 1) * DV)
            order += [q[..., c1], k[..., c1], v[..., c2], o[..., c2], mg[..., br * D + h * DV:br * D + (h + 1) * DV]]
    for j in range(KT // 2):
        c2 = slice(j * 2 * P, (j + 1) * 2 * P)
        order += [lx[..., c2], ly[..., c2], mg[..., 2 * D + j * 2 * P:2 * D + (j + 1) * 2 * P]]
    out["w_mix"] = blocks(np.concatenate(order, axis=2))
    gw = np.zeros((DEPTH, D, P), f)
    gw[:, :, 0:HEADS], gw[:, :, 32:32 + HEADS], gw[:, :, 64:80] = mif[..., :HEADS], mif[..., HEADS:], glr_
    out["w_gates"] = gw.reshape(DEPTH, KT, P, P).transpose(0, 2, 1, 3).reshape(DEPTH, P, GATE_W)
    out["w_o"] = blocks(a["w_out"])

    def feat(v):
        return v.reshape(DEPTH, -1, P).transpose(0, 2, 1)

    nxt = np.stack([a["norm_ffn1"][l + 1] if l + 1 < DEPTH else a["norm_final"] for l in range(DEPTH)])
    conv = a["w_conv"].reshape(DEPTH, 4 * D)
    per = np.concatenate([feat(v) for v in (a["norm_mix"], a["norm_ffn2"], nxt, a["g_ml_norm"], a["g_gla_norm"], conv,
                                            a["b_conv"], a["b_lru_a"], a["b_lru_i"], a["lru_lambda"],
                                            a["b_gla_gate"])], axis=2)
    out["vec"] = np.concatenate([per[l] for l in range(DEPTH)] + [a["norm_ffn1"][0].reshape(KT, P).T], axis=1)
    out["b_if"] = a["b_ml_if"].reshape(DEPTH, 2, HEADS).transpose(2, 0, 1)
    out["w_lr2"] = a["w_gla_lr2"].reshape(DEPTH, r16, HEADS, DK).transpose(0, 2, 1, 3)
    for n_, w in (("w_ra", a["w_lru_a"]), ("w_ri", a["w_lru_i"])):
        out[n_] = w.reshape(DEPTH, 2, KT // 2, P, P).transpose(0, 1, 3, 2, 4)
    s, t = np.arange(P)[:, None], np.arange(P)[None, :]
    c = np.zeros((P, 2 * P + P + NS + SEQS + N), f)
    c[:, 0:P], c[:, P:2 * P] = np.eye(P), 1
    c[:, 2 * P:3 * P] = np.where(s <= t, 0, NEG)
    s4, t4 = np.arange(NS)[:, None], np.arange(NS)[None, :]
    o = 3 * P
    c[0:NS, o:o + NS] = np.where((s4 <= t4) & (s4 // TS == t4 // TS), 0, NEG)
    c[0:NS, o + NS:o + NS + SEQS] = s4 // TS == np.arange(SEQS)[None, :]
    tok = np.arange(N)
    c[:, o + NS + SEQS:] = np.where(tok < T, tok % C != 0, (tok - T) % TS != 0)
    out["consts"] = c
    out["level_masks"] = np.stack([(s // (2 * h) == t // (2 * h)) & (s % (2 * h) < h) & (t % (2 * h) >= h)
                                   for h in LEVELS], axis=1).astype(np.int32)
    out["m0"] = a["state_mlstm_m"].transpose(2, 0, 1)
    out["c0"] = a["state_mlstm_C"].transpose(0, 2, 4, 1, 3)
    out["n0"] = a["state_mlstm_n"].transpose(0, 2, 3, 1)
    out["s0"] = a["state_gla_S"].transpose(0, 2, 3, 1, 4)
    out["h0"] = a["state_lru_h"].reshape(DEPTH, SEQS, KT, P).transpose(0, 3, 2, 1)
    out["conv0"] = a["state_lru_conv"].reshape(DEPTH, SEQS, 3, KT, P).transpose(0, 4, 3, 1, 2)
    return {k: np.ascontiguousarray(v) for k, v in out.items()}


_OUTS = {
    "o_y": (P, KT, N), "o_pc": (DEPTH, HEADS, P, DV + 1), "o_pm": (DEPTH, HEADS, 1), "o_ps": (DEPTH, HEADS, P, DV),
    "o_ph": (DEPTH, P, KT), "o_pconv": (DEPTH, P, KT, 3), "o_sc": (DEPTH, HEADS, P, SEQS, DV),
    "o_sn": (DEPTH, HEADS, P, SEQS), "o_sm": (DEPTH, HEADS, SEQS), "o_ss": (DEPTH, HEADS, P, SEQS, DV),
    "o_sh": (DEPTH, P, KT, SEQS), "o_sconv": (DEPTH, P, KT, SEQS, 3),
}


def kernel(**inputs):
    import numpy as np
    import concourse.bacc as bacc
    from concourse import mybir as mb
    from concourse.bass_utils import run_bass_kernel_spmd as run

    nc = bacc.Bacc("TRN2", target_bir_lowering=False, num_devices=1)
    arrays, args = {}, {}
    for name, v in _layout(inputs).items():
        arrays[f"in_{name}"] = v
        args[name] = nc.dram_tensor(f"in_{name}", v.shape, mb.dt.from_np(v.dtype), kind="ExternalInput").ap()
    for name, shape in _OUTS.items():
        args[name] = nc.dram_tensor(f"out_{name}", shape, mb.dt.float32, kind="ExternalOutput").ap()
    args["rows_dram"] = nc.dram_tensor("rows_scratch", (HEADS, 4 * N), mb.dt.float32, kind="Internal").ap()
    trunk(nc, **args)
    r = run(nc, [arrays], core_ids=[0]).results[0]
    o = {name: np.asarray(r[f"out_{name}"]) for name in _OUTS}

    y = o["o_y"].transpose(2, 1, 0).reshape(N, D)
    pc = o["o_pc"]
    got = (
        y[:T][None], y[T:].reshape(SEQS, TS, D),
        pc[..., :DV].transpose(0, 1, 3, 2)[:, None], pc[..., DV][:, None], o["o_pm"][:, None, :, 0],
        o["o_ps"][:, None], o["o_ph"].transpose(0, 2, 1).reshape(DEPTH, 1, D),
        o["o_pconv"].transpose(0, 3, 2, 1).reshape(DEPTH, 1, 3, D),
        o["o_sc"].transpose(0, 3, 1, 4, 2), o["o_sn"].transpose(0, 3, 1, 2), o["o_sm"].transpose(0, 2, 1),
        o["o_ss"].transpose(0, 3, 1, 2, 4), o["o_sh"].transpose(0, 3, 2, 1).reshape(DEPTH, SEQS, D),
        o["o_sconv"].transpose(0, 3, 4, 2, 1).reshape(DEPTH, SEQS, 3, D),
    )
    return tuple(np.ascontiguousarray(v) for v in got)
```

```python
from contextlib import ExitStack

import concourse.bass as bass
from concourse import mybir

F32 = mybir.dt.float32
F32R = mybir.dt.float32r
I32 = mybir.dt.int32
ALU = mybir.AluOpType
ACT = mybir.ActivationFunctionType
ds = bass.ds

P = 128
D = 1024
KT = D // P
DEPTH = 2
T = 512
SEQS, TS = 8, 4
NS = SEQS * TS
N = T + NS
HALF = N // 2
FF = 2816
HEADS = 4
DK = 128
DV = D // HEADS
C = 128
NC = T // C
EPS = 1e-6
NEG = -1e30
LEVELS = [64, 32, 16, 8, 4, 2, 1]
NL = len(LEVELS)
NLS = 2

FF_HALVES = [12, 10]
assert sum(FF_HALVES) * P == FF
W_SLOT = 2048

FFN_BLOCKS = sum(FF_HALVES) + 2 * KT
FFN_TILES = 2 * sum(FF_HALVES) + 2 * KT
HEAD_BLOCKS, HEAD_TILES = 4, 8
LRU_BLOCKS, LRU_TILES = 3, 6
MIX_BLOCKS = 2 * HEADS * HEAD_BLOCKS + KT // 2 * LRU_BLOCKS
GATE_TILES = 2
MIX_TILES = GATE_TILES + 2 * HEADS * HEAD_TILES + KT // 2 * LRU_TILES
OUT_BLOCKS, OUT_TILES = KT // 2, KT
BLK_MIX = FFN_BLOCKS
BLK_OUT = BLK_MIX + MIX_BLOCKS
BLK_FFN2 = BLK_OUT + OUT_BLOCKS
LAYER_BLOCKS = BLK_FFN2 + FFN_BLOCKS
TILE_MIX = FFN_TILES
TILE_OUT = TILE_MIX + MIX_TILES
TILE_FFN2 = TILE_OUT + OUT_TILES
LAYER_TILES = TILE_FFN2 + FFN_TILES

V_MIX, V_FFN2, V_NEXT, V_GML, V_GGLA = 0, 8, 16, 24, 32
V_CONV, V_BCONV, V_BA, V_BI, V_LAM, V_BGLA = 40, 72, 80, 88, 96, 104
V_COLS = 108
V_FIRST = DEPTH * V_COLS
V_ALL = V_FIRST + KT
GATE_W = KT * P
STORES = 2 + HEADS * 3 + HEADS * 2 + 4


def spread(ap, dim, n):
    shape = list(ap.shape)
    shape[dim] = n
    return ap.broadcast_to(shape)


class Chain:

    def __init__(self, eng, sem, ready):
        self.eng, self.sem, self.ready, self.n = eng, sem, ready, 0
        self.spare = eng.alloc_register(f"{sem.name}_spare")
        eng.reg_mov(self.spare, 1)

    def hold(self):
        self.eng.reg_alu(self.spare, self.spare, 1, ALU.max)

    def end(self):
        self.eng.wait_ge(self.ready, self.spare)

    def restart(self):
        self.hold()
        self.eng.sem_clear(self.sem)
        self.n = 0

    def link(self, ins):
        self.n += 1
        ins.then_inc(self.sem, 1)
        self.eng.wait_ge(self.sem, self.n)


CONST_LOADS = 10


def trunk(nc, x_T, w_up1, w_down1, w_mix, w_gates, w_o, w_up2, w_down2, vec, b_if, w_lr2, w_ra, w_ri, consts, level_masks,
          m0, c0, n0, s0, h0, conv0, o_y, o_pc, o_pm, o_ps, o_ph, o_pconv,
          o_sc, o_sn, o_sm, o_ss, o_sh, o_sconv, rows_dram):
    with ExitStack() as ctx:
        def sb(name, shape, dt=F32, where=ctx):
            return where.enter_context(nc.sbuf_tensor(name, shape, dt))

        def sem(name):
            return ctx.enter_context(nc.semaphore(name))

        x = sb("x", [P, KT, N])
        xh = sb("xh", [P, KT, N], F32R)
        xl = sb("xl", [P, KT, N], F32R)
        stage = sb("stage", [P, 2, W_SLOT])
        wh = sb("wh", [P, 2, W_SLOT], F32R)
        wl = sb("wl", [P, 2, W_SLOT], F32R)
        gstage = sb("gstage", [P, GATE_W])
        V = sb("vectors", [P, V_ALL])
        ones = sb("ones", [P, P])
        ident = sb("ident", [P, P])
        eps_t = sb("eps_t", [P, 1])
        one_t = sb("one_t", [P, 1])
        zero_t = sb("zero_t", [P, 1])
        acc = sb("acc", [P, N])
        sq = sb("sq", [P, N])
        xg = sb("xg", [P, N])
        sd = sb("sd", [P, N])
        rstd = sb("rstd", [P, N])
        sdT = sb("sdT", [P, 5])
        rstdT = sb("rstdT", [P, 5])
        c8 = sb("c8", [P, DEPTH * KT])
        nc8 = sb("nc8", [P, DEPTH * KT])
        masks = sb("masks", [P, NL, P], I32)
        neg_p = sb("neg_p", [P, P])
        neg_s = sb("neg_s", [NS, NS])
        seqm = sb("seqm", [NS, SEQS])
        reset = sb("reset", [P, N])
        bif = sb("bif", [HEADS, DEPTH, 2])
        m0t = sb("m0t", [HEADS, DEPTH, SEQS])
        t8 = sb("t8", [P, SEQS])
        m_out = sb("m_out", [HEADS, 1 + SEQS])
        ff = ExitStack()
        hh = sb("hh", [P, FF_HALVES[0], N], F32R, ff)
        hl = sb("hl", [P, FF_HALVES[0], N], F32R, ff)
        gs = sb("gs", [P, N], where=ff)
        us = sb("us", [P, N], where=ff)
        sg = sb("sg", [P, N], where=ff)
        hp = sb("hp", [P, N], where=ff)
        ff.close()
        merged = sb("merged", [P, KT, N])
        heads = ExitStack()
        gwh = sb("gwh", [P, GATE_W], F32R, heads)
        gwl = sb("gwl", [P, GATE_W], F32R, heads)
        heads.close()
        heads = ExitStack()
        qT = sb("qT", [P, N], where=heads)
        kT = sb("kT", [P, N], where=heads)
        qs = sb("qs", [P, N], where=heads)
        val = sb("val", [P, NC + 1, DV + P], where=heads)
        seven = sb("seven", [P, NL, N], where=heads)
        wS = sb("wS", [P, N], where=heads)
        Kw = sb("Kw", [P, NC, P], where=heads)
        Kts = sb("Kts", [NS, P], where=heads)
        Kws = sb("Kws", [NS, SEQS, P], where=heads)
        Cst = sb("Cst", [P, NC, DV + P], where=heads)
        CS = sb("CS", [P, SEQS, DV], where=heads)
        nS = sb("nS", [P, 2, SEQS], where=heads)
        qn = sb("qn", [P, NS], where=heads)
        hsq = sb("hsq", [P, 2, N], where=heads)
        Hh = sb("Hh", [P, 2, N], where=heads)
        Gm = sb("Gm", [P, 2, N], where=heads)
        tg = sb("tg", [P, N], where=heads)
        cols = sb("cols", [P, 8], where=heads)
        lr2 = sb("lr2", [P, P], where=heads)
        heads.close()
        lru = ExitStack()
        mh = sb("mh", [P, KT, N], F32R, lru)
        ml = sb("ml", [P, KT, N], F32R, lru)
        lxp = sb("lxp", [P, 2, T + 3], where=lru)
        lxs = sb("lxs", [P, 2, SEQS, TS + 3], where=lru)
        xc = sb("xc", [P, 2, N], where=lru)
        rr = sb("rr", [P, N], where=lru)
        ii = sb("ii", [P, N], where=lru)
        aa = sb("aa", [P, N], where=lru)
        tt = sb("tt", [P, N], where=lru)
        hseq = sb("hseq", [P, 2, N], where=lru)
        lyg = sb("lyg", [P, 2, N], where=lru)
        wra = sb("wra", [P, KT // 2, P], where=lru)
        wri = sb("wri", [P, KT // 2, P], where=lru)
        h0t = sb("h0t", [P, KT, SEQS], where=lru)
        cv0 = sb("cv0", [P, KT, SEQS, 3], where=lru)
        ph = sb("ph", [P, KT], where=lru)
        sh = sb("sh", [P, KT, SEQS], where=lru)
        pcv = sb("pcv", [P, KT, 3], where=lru)
        scv = sb("scv", [P, KT, SEQS, 3], where=lru)
        lru.close()

        def psum(name, shape):
            return ctx.enter_context(nc.psum_tensor(name, shape, F32))

        pair = [psum("stream_a", [P, 2, 512]), psum("stream_b", [P, 2, 512])]
        Q = psum("mix", [P, 4, 512])

        const_loaded = sem("const_loaded")
        x_loaded = sem("x_loaded")
        block_loaded = [sem("block_loaded_0"), sem("block_loaded_1")]
        split_done = sem("split_done")
        tile_done = sem("tile_done")
        tile_free = sem("tile_free")
        silu_done = sem("silu_done")
        h_done = sem("h_done")
        sq_ready = sem("sq_ready")
        acc_ready = sem("acc_ready")
        norm_sum = sem("norm_sum")
        sd_ready = sem("sd_ready")
        c8_ready = sem("c8_ready")
        c8_in = sem("c8_in")
        gate_loaded = sem("gate_loaded")
        gate_split = sem("gate_split")
        gate_in = sem("gate_in")
        gate_ln = sem("gate_ln")
        rows_ready = sem("rows_ready")
        rows_stored = sem("rows_stored")
        root_done = sem("root_done")
        head_samples = sem("head_samples")
        heads_done = sem("heads_done")
        state_stored = sem("state_stored")
        gate_act = sem("gate_act")
        dve_chain, act_chain, pool_chain = sem("dve_chain"), sem("act_chain"), sem("pool_chain")
        init_done = sem("init_done")
        a_rows = sem("a_rows_loaded")
        a_cs = sem("a_state_loaded")
        a_si, a_exin, a_ex = sem("a_si"), sem("a_exp_in"), sem("a_exp")
        a_scores, a_kw, a_u, a_c = sem("a_scores"), sem("a_weights"), sem("a_update"), sem("a_state")
        a_den, a_out, a_h, a_us = sem("a_denominator"), sem("a_out"), sem("a_h"), sem("a_sample_update")
        a_mean, a_hc, a_sq, a_sqs = sem("a_mean"), sem("a_centred"), sem("a_squares"), sem("a_square_sum")
        a_var = sem("a_var")
        b_lr, b_cs = sem("b_lr_loaded"), sem("b_state_loaded")
        b_z, b_zin, b_ln, b_diff, b_exp = sem("b_z"), sem("b_z_in"), sem("b_ln"), sem("b_diff"), sem("b_exp")
        b_fac, b_ring, b_took = sem("b_factors"), sem("b_ring_full"), sem("b_ring_took")
        b_u, b_c, b_out, b_h = sem("b_update"), sem("b_state"), sem("b_out"), sem("b_h")
        b_us, b_sq, b_sqs, b_var = sem("b_sample_update"), sem("b_squares"), sem("b_square_sum"), sem("b_var")
        l_vec, l_w = sem("l_vectors_loaded"), sem("l_weights_loaded")
        l_xc, l_ri, l_sig, l_at, l_min, l_mult = (sem("l_conv"), sem("l_gates"), sem("l_sigmoids"), sem("l_decay"),
                                                  sem("l_mult_in"), sem("l_mult"))
        l_act = sem("l_act")
        m_ready = sem("m_ready")
        lru_done = sem("lru_done")
        y_ready = sem("y_ready")
        y_stored = sem("y_stored")

        RB, SI, EM, Ex = seven[:, 0:4, :], seven[:, 4, :], seven[:, 5, :], seven[:, 6, :]
        glr = xg[64:80, :]
        kh, bc, eb = sq, acc, sd

        def halves(ap):
            return ap.rearrange("p (a b) -> p a b", a=2)

        def banks(p):
            return p[:, :, 0:HALF]

        block = ctx.enter_context(nc.Block())

        @block.sync
        def _(sp):
            sp.dma_start(V[:], vec).then_inc(const_loaded, 16)
            sp.dma_start(x[:], x_T).then_inc(x_loaded, 16)

            def load(n, slot, src):
                sp.wait_ge(split_done, n + 1)
                width = src.shape[1]
                sp.dma_start(stage[:, slot, 0:width], src).then_inc(block_loaded[slot], 16)

            def ffn(L, first, w_up, w_down):
                n = L * LAYER_BLOCKS + first
                up = down = 0
                for tiles in FF_HALVES:
                    with sp.Fori(0, tiles // 2) as i:
                        for j in range(2):
                            load(i * 2 + (n + j), j, w_up[L, i * 2 + (up + j)])
                    n = n + tiles
                    up += tiles
                    with sp.Fori(0, KT // 2) as i:
                        for j in range(2):
                            load(i * 2 + (n + j), j, w_down[L, i * 2 + (down + j), :, 0:tiles * P])
                    n = n + KT
                    down += KT

            sp.wait_ge(init_done, 1)
            with sp.Fori(0, DEPTH) as L:
                ffn(L, 0, w_up1, w_down1)
                sp.dma_start(gstage[:], w_gates[L]).then_inc(gate_loaded, 16)
                with sp.Fori(0, MIX_BLOCKS // 2) as i:
                    for j in range(2):
                        load(L * LAYER_BLOCKS + i * 2 + (BLK_MIX + j), j, w_mix[L, i * 2 + j])
                with sp.Fori(0, OUT_BLOCKS // 2) as i:
                    for j in range(2):
                        load(L * LAYER_BLOCKS + i * 2 + (BLK_OUT + j), j, w_o[L, i * 2 + j])
                ffn(L, BLK_FFN2, w_up2, w_down2)
            for m in range(KT):
                sp.wait_ge(y_ready, m + 1)
                sp.dma_start(o_y[:, m, :], x[:, m, :]).then_inc(y_stored, 16)
            sp.wait_ge(y_stored, 16 * KT)
            sp.wait_ge(state_stored, 16 * DEPTH * STORES)

        @block.gpsimd
        def _(pool):
            chain = Chain(pool, pool_chain, init_done)
            pool.memset(eps_t[:], EPS)
            pool.memset(zero_t[:], 0.0)
            pool.memset(one_t[:], 1.0).then_inc(split_done, 2)
            pool.memset(rstdT[:], 1.0).then_inc(tile_done, 2)
            pool.memset(sdT[:], 1.0).then_inc(init_done, 1)

            def split(half_n, through, slot, width):
                pool.wait_ge(block_loaded[slot], half_n * 16 + 16)
                pool.wait_ge(tile_done, through + 2)
                chain.hold()
                w = stage[:, slot, 0:width]
                chain.link(pool.tensor_tensor(wh[:, slot, 0:width], w, spread(zero_t[:], 1, width), ALU.add))
                pool.tensor_tensor(wl[:, slot, 0:width], stage[:, slot, 0:width],
                                   wh[:, slot, 0:width].bitcast(F32), ALU.subtract).then_inc(split_done, 1)

            def run(L, first, blocks, width, first_tile, tiles_each, ahead, before=None):
                half = L * (LAYER_BLOCKS // 2) + first // 2
                t = L * LAYER_TILES + first_tile
                last = t if before is None else L * LAYER_TILES + before
                chain.restart()
                split(half, last - ahead, 0, width)
                split(half, last, 1, width)
                with pool.Fori(1, blocks // 2) as i:
                    chain.restart()
                    for j in range(2):
                        split(half + i, t + (i * 2 + (j - 1)) * tiles_each, j, width)

            def ffn(L, first, first_tile, ahead):
                for tiles in FF_HALVES:
                    run(L, first, tiles, 2 * D, first_tile, 2, ahead)
                    run(L, first + tiles, KT, tiles * P, first_tile + 2 * tiles, 1, 2)
                    ahead = 1
                    first += tiles + KT
                    first_tile += 2 * tiles + KT

            pool.wait_ge(init_done, 1)
            with pool.Fori(0, DEPTH) as L:
                ffn(L, 0, 0, 1)
                pool.wait_ge(gate_loaded, L * 16 + 16)
                pool.wait_ge(tile_done, L * LAYER_TILES + FFN_TILES + 2)
                chain.restart()
                chain.link(pool.tensor_tensor(gwh[:], gstage[:], spread(zero_t[:], 1, GATE_W), ALU.add))
                pool.tensor_tensor(gwl[:], gstage[:], gwh[:].bitcast(F32), ALU.subtract).then_inc(gate_split, 1)
                run(L, BLK_MIX, MIX_BLOCKS, 2 * D, TILE_MIX + GATE_TILES, 2, 1, before=FFN_TILES)
                run(L, BLK_OUT, OUT_BLOCKS, 2 * D, TILE_OUT, 2, 2)
                ffn(L, BLK_FFN2, TILE_FFN2, 2)
            chain.end()

        @block.tensor
        def _(pe):
            def three_pass(out, lhs, rhs, first, last):
                (lh, ll), (rh, rl) = lhs, rhs
                for a, b, f, z in ((lh, rh, first, False), (ll, rh, False, False), (lh, rl, False, last)):
                    mm = [pe.matmul(out(h), a(h), b(h), start=f, stop=z) for h in range(2)]
                return mm[-1]

            def block_ready(n):
                pe.wait_ge(split_done, n + 3)

            def tile(t, slot, k_tiles, width, col, act=(xh, xl), weights=(wh, wl), late=None, fresh=None,
                     count=1):
                p = pair[slot]
                pe.wait_ge(tile_free, t + 1)
                for k in range(k_tiles):
                    if late and k == k_tiles - 1:
                        late()
                    if fresh is not None:
                        pe.wait_ge(acc_ready, fresh - (k_tiles - 1 - k))
                    c0_ = k * width + col
                    mm = three_pass(lambda h: p[:, h, 0:HALF],
                                    [lambda h, w=w: w[:, c0_:c0_ + P] for w in weights],
                                    [lambda h, a=a: a[:, k, h * HALF:(h + 1) * HALF] for a in act],
                                    k == 0, k == k_tiles - 1)
                mm.then_inc(tile_done, count)

            def norm_squares():
                for h in range(2):
                    mm = pe.matmul(Q[:, h, 0:HALF], ones[:], acc[:, h * HALF:(h + 1) * HALF], start=True, stop=True)
                return mm

            def ffn_in_block(L, n, t, j, norm=None):
                block_ready(n)
                tile(t, 0, KT, 2 * P, 0, weights=(wh[:, j], wl[:, j]), fresh=norm)
                if norm is not None:
                    pe.wait_ge(acc_ready, norm)
                    norm_squares().then_inc(norm_sum, 1)
                tile(t + 1, 1, KT, 2 * P, P, weights=(wh[:, j], wl[:, j]))

            def ffn(L, first, first_tile, h_base, norm):
                n = L * LAYER_BLOCKS + first
                t = L * LAYER_TILES + first_tile
                hd = L * (2 * sum(FF_HALVES)) + h_base
                for half, tiles in enumerate(FF_HALVES):
                    start = 0
                    if half == 0:
                        for j in range(2):
                            ffn_in_block(L, n + j, t + 2 * j, j, norm if j == 0 else None)
                        start = 1
                    with pe.Fori(start, tiles // 2) as i:
                        for j in range(2):
                            ffn_in_block(L, i * 2 + (n + j), i * 4 + (t + 2 * j), j)
                    n, t, hd = n + tiles, t + 2 * tiles, hd + tiles
                    with pe.Fori(0, KT // 2) as i:
                        for j in range(2):
                            block_ready(i * 2 + (n + j))
                            pe.wait_ge(h_done, hd - 1)
                            tile(i * 2 + (t + j), j, tiles, P, 0, act=(hh, hl), weights=(wh[:, j], wl[:, j]),
                                 late=lambda: pe.wait_ge(h_done, hd))
                    n, t = n + KT, t + KT

            def value_tiles(t, j):
                for which, starts in enumerate(([c * C for c in range(NC)], [N - C])):
                    pe.wait_ge(tile_free, t + which + 1)
                    for c, tok in enumerate(starts):
                        out = pair[which][:, c // 2, c % 2 * DV:(c % 2 + 1) * DV]
                        for k in range(KT):
                            for a, b, f, z in ((xh, wh, k == 0, False), (xl, wh, False, False),
                                               (xh, wl, False, k == KT - 1)):
                                mm = pe.matmul(out, a[:, k, tok:tok + C], b[:, j, k * DV:(k + 1) * DV],
                                               start=f, stop=z)
                    mm.then_inc(tile_done, 1)

            def pair_block(n, t, j, after_first=None):
                block_ready(n)
                tile(t, 0, KT, 2 * P, 0, weights=(wh[:, j], wl[:, j]))
                if after_first:
                    after_first()
                tile(t + 1, 1, KT, 2 * P, P, weights=(wh[:, j], wl[:, j]))

            def gate_block(L):
                pe.wait_ge(gate_split, L + 1)
                tile(L * LAYER_TILES + TILE_MIX, 0, KT, P, 0, weights=(gwh, gwl), count=GATE_TILES,
                     fresh=L * (3 * KT) + 2 * KT)
                pe.wait_ge(acc_ready, L * (3 * KT) + 2 * KT)
                norm_squares()
                for c in range(NC + 1):
                    tok = c * C if c < NC else N - C
                    mm = pe.matmul(Q[:, 2, c:c + 1], acc[:, tok:tok + C], ones[:, 0:1], start=True, stop=True)
                mm.then_inc(norm_sum, 1)

            def sample_states(b_, v, out_col, lhs_of):
                for s_ in range(SEQS):
                    mm = pe.matmul(Q[:, b_, out_col + s_ * TS:out_col + (s_ + 1) * TS], lhs_of(s_, v),
                                   qs[:, T + s_ * TS:T + (s_ + 1) * TS], start=False, stop=s_ == SEQS - 1,
                                   skip_group_check=True)
                return mm

            def sample_updates(half, done):
                for e in range(SEQS // 2):
                    mm = pe.matmul(Q[:, 2 + e // 2, e % 2 * DV:(e % 2 + 1) * DV], Kws[:, half * SEQS // 2 + e, :],
                                   val[0:NS, NC, 0:DV], start=True, stop=True)
                mm.then_inc(done, 1)

            def column_sum(src, b_, done):
                for h in range(2):
                    mm = pe.matmul(Q[:, b_ + h, 0:HALF], ones[:], src[:, h * HALF:(h + 1) * HALF], start=True, stop=True)
                mm.then_inc(done, 1)

            def mlstm_head(L, i):
                B = L * HEADS + i
                n = L * LAYER_BLOCKS + i * HEAD_BLOCKS + BLK_MIX
                t = L * LAYER_TILES + i * HEAD_TILES + (TILE_MIX + GATE_TILES)
                pair_block(n, t, 0)
                block_ready(n + 1)
                value_tiles(t + 2, 1)
                pe.wait_ge(tile_free, t + 6)
                pe.wait_ge(a_rows, B * 16 + 16)
                pe.wait_ge(root_done, L * (2 * HEADS) + i + 1)
                pe.wait_ge(head_samples, L * (4 * HEADS) + i * 2 + 1)
                for c in range(NC):
                    sl = slice(c * C, (c + 1) * C)
                    pe.matmul(Q[:, 0, sl], kT[:, sl], qT[:, sl], start=True, stop=True)
                for c in range(NC):
                    sl = slice(c * C, (c + 1) * C)
                    pe.transpose(Q[:, 1, sl], kT[:, sl], ident[:])
                sm = slice(T, N)
                pe.matmul(Q[0:NS, 2, 0:NS], kT[:, sm], qT[:, sm], start=True, stop=True)
                pe.transpose(Q[0:NS, 2, NS:NS + P], kT[:, sm], ident[:])
                for c in range(NC + 1):
                    m = C if c < NC else NS
                    mm = pe.matmul(Q[0:m, 2, 200 + c:201 + c], RB[0:1, 3, c * C:c * C + m], ones[0:1, 0:1],
                                   start=True, stop=True)
                mm.then_inc(a_scores, 1)

                def updates():
                    pe.wait_ge(a_kw, B + 1)
                    for c in range(NC):
                        pe.matmul(Q[:, c, 0:DV + P], Kw[:, c, :], val[:, c, :], start=True, stop=True).then_inc(a_u, 1)

                pair_block(n + 2, t + 4, 0, updates)

                def over_chunks(v):
                    vs = slice(v * P, (v + 1) * P)
                    for c in range(NC):
                        sl = slice(c * C, (c + 1) * C)
                        mm = pe.matmul(Q[:, v, sl], val[:, c, vs], wS[:, sl], start=True, stop=c == 0)
                        if c:
                            mm = pe.matmul(Q[:, v, sl], Cst[:, c - 1, vs], qs[:, sl], start=False, stop=True)
                    return mm

                pe.wait_ge(a_c, B * NC + NC)
                over_chunks(2)
                pe.wait_ge(a_cs, B * 32 + 32)
                for v in range(3):
                    pe.matmul(Q[:, 3, v * NS:(v + 1) * NS], val[0:NS, NC, v * P:(v + 1) * P], wS[0:NS, sm],
                              start=True, stop=False, skip_group_check=True)
                    if v < 2:
                        sample_states(3, v, v * NS, lambda s_, v_: CS[:, s_, v_ * P:(v_ + 1) * P])
                pe.matmul(Q[:, 3, 2 * NS:3 * NS], ones[:], qn[:], start=False, stop=True, skip_group_check=True)
                pe.matmul(Q[:, 3, 3 * NS:3 * NS + SEQS], Kts[:], Ex[0:NS, T + TS - 1:N:TS],
                          start=True, stop=True).then_inc(a_den, 1)
                over_chunks(0)
                over_chunks(1).then_inc(a_out, 1)

                def mean():
                    pe.wait_ge(a_h, B + 1)
                    column_sum(wS, 0, a_mean)
                    sample_updates(0, a_us)

                pair_block(n + 3, t + 6, 1, mean)
                pe.wait_ge(a_sqs, B + 1)
                column_sum(hsq[:, 0], 0, a_var)
                pe.wait_ge(head_samples, L * (4 * HEADS) + i * 2 + 2)
                sample_updates(1, a_us)

            def gla_head(L, i):
                B = L * HEADS + i
                n = L * LAYER_BLOCKS + i * HEAD_BLOCKS + (BLK_MIX + HEADS * HEAD_BLOCKS)
                t = L * LAYER_TILES + i * HEAD_TILES + (TILE_MIX + GATE_TILES + HEADS * HEAD_TILES)
                pe.wait_ge(b_lr, B * 16 + 16)
                pe.wait_ge(root_done, L * (2 * HEADS) + HEADS + 1 + i)
                for h in range(2):
                    mm = pe.matmul(Q[:, h, 0:HALF], lr2[64:80, :], xg[64:80, h * HALF:(h + 1) * HALF],
                                   start=True, stop=True)
                mm.then_inc(b_z, 1)
                pair_block(n, t, 0)
                block_ready(n + 1)
                value_tiles(t + 2, 1)
                sm = slice(T, N)

                def ring(r):
                    if r >= 4:
                        pe.wait_ge(b_took, B * 10 + (r - 3))
                    return r % 4

                def scores():
                    pe.wait_ge(b_fac, B + 1)
                    for r in range(NL + 1):
                        q = ring(r)
                        for c in range(NC):
                            sl = slice(c * C, (c + 1) * C)
                            lhs, rhs = (kT[:, sl], qT[:, sl]) if r == 0 else (seven[:, r - 1, sl], seven[:, r - 1, sl])
                            mm = pe.matmul(Q[:, q, sl], lhs, rhs, start=True, stop=True)
                        mm.then_inc(b_ring, 1)
                    q = ring(NL + 1)
                    for c in range(NC):
                        sl = slice(c * C, (c + 1) * C)
                        mm = pe.transpose(Q[:, q, sl], kh[:, sl], ident[:])
                    mm.then_inc(b_ring, 1)
                    q = ring(NL + 2)
                    pe.transpose(Q[0:NS, q, P:2 * P], kh[:, sm], ident[:])
                    pe.matmul(Q[0:NS, q, 0:NS], kT[:, sm], qT[:, sm], start=True, stop=True)
                    for e in range(NLS):
                        lv = seven[:, NL - NLS + e, sm]
                        mm = pe.matmul(Q[0:NS, q, (e + 1) * NS:(e + 2) * NS], lv, lv, start=True, stop=True)
                    mm.then_inc(b_ring, 1)

                pair_block(n + 2, t + 4, 0, scores)
                pe.wait_ge(b_took, B * 10 + 10)
                for c in range(NC):
                    pe.matmul(Q[:, c, 0:DV], Kw[:, c, :], val[:, c, 0:DV], start=True, stop=True).then_inc(b_u, 1)

                def outputs():
                    pe.wait_ge(b_c, B * NC + NC)
                    for v in range(2):
                        vs = slice(v * P, (v + 1) * P)
                        for c in range(NC):
                            sl = slice(c * C, (c + 1) * C)
                            pe.matmul(Q[:, v, sl], val[:, c, vs], wS[:, sl], start=True, stop=c == 0)
                            if c:
                                pe.matmul(Q[:, v, sl], Cst[:, c - 1, vs], qs[:, sl], start=False, stop=True)
                    pe.wait_ge(b_cs, B * 16 + 16)
                    for v in range(2):
                        pe.matmul(Q[:, 2, v * NS:(v + 1) * NS], val[0:NS, NC, v * P:(v + 1) * P], wS[0:NS, sm],
                                  start=True, stop=False, skip_group_check=True)
                        mm = sample_states(2, v, v * NS, lambda s_, v_: CS[:, s_, v_ * P:(v_ + 1) * P])
                    mm.then_inc(b_out, 1)

                pair_block(n + 3, t + 6, 1, outputs)
                pe.wait_ge(b_sqs, B + 1)
                column_sum(hsq[:, 0], 0, b_var)
                sample_updates(0, b_us)
                pe.wait_ge(head_samples, L * (4 * HEADS) + i * 2 + (2 * HEADS + 2))
                sample_updates(1, b_us)

            def lru_pair(L, i, j2):
                pr = L * (KT // 2) + i * 2 + j2
                n = L * LAYER_BLOCKS + i * 6 + (BLK_MIX + 2 * HEADS * HEAD_BLOCKS + 3 * j2)
                t = L * LAYER_TILES + i * 12 + (TILE_MIX + GATE_TILES + 2 * HEADS * HEAD_TILES + 6 * j2)

                def gates(j):
                    if j2 == 0 and j == 0:
                        pe.wait_ge(l_w, L * 64 + i * 32 + 32)
                    pe.wait_ge(l_xc, pr * 2 + (j + 1))
                    pe.wait_ge(l_sig, pr * 2 + (j + 1))
                    for w_, b_ in ((wra, 0), (wri, 2)):
                        for h in range(2):
                            mm = pe.matmul(Q[:, b_ + h, 0:HALF], w_[:, 2 * j2 + j, :], xc[:, j, h * HALF:(h + 1) * HALF],
                                           start=True, stop=True)
                    mm.then_inc(l_ri, 1)

                s0_ = j2 % 2
                pair_block(n, t, s0_)
                gates(0)
                pair_block(n + 1, t + 2, 1 - s0_, lambda: gates(1))
                pair_block(n + 2, t + 4, s0_)

            pe.wait_ge(const_loaded, 16 * CONST_LOADS)
            with pe.Fori(0, DEPTH) as L:
                ffn(L, 0, 0, 0, L * (3 * KT) + KT)
                gate_block(L)
                with pe.Fori(0, HEADS) as i:
                    mlstm_head(L, i)
                with pe.Fori(0, HEADS) as i:
                    gla_head(L, i)
                with pe.Fori(0, KT // 4) as i:
                    lru_pair(L, i, 0)
                    lru_pair(L, i, 1)
                with pe.Fori(0, OUT_BLOCKS // 2) as i:
                    for j in range(2):
                        n = L * LAYER_BLOCKS + i * 2 + (BLK_OUT + j)
                        t = L * LAYER_TILES + i * 4 + (TILE_OUT + 2 * j)
                        block_ready(n)
                        pe.wait_ge(m_ready, L * KT + (KT - 1))
                        for e in range(2):
                            tile(t + e, e, KT, 2 * P, e * P, act=(mh, ml), weights=(wh[:, j], wl[:, j]),
                                 late=lambda: pe.wait_ge(m_ready, L * KT + KT))
                ffn(L, BLK_FFN2, TILE_FFN2, sum(FF_HALVES), L * (3 * KT) + 3 * KT)
            pe.wait_ge(acc_ready, DEPTH * 3 * KT + KT)
            norm_squares().then_inc(norm_sum, 1)

        @block.scalar
        def _(act):
            chain = Chain(act, act_chain, init_done)

            col = 0
            for dst in (ident, ones, neg_p, neg_s, seqm, reset):
                width = dst.shape[1]
                act.dma_start(dst[:], consts[0:dst.shape[0], col:col + width]).then_inc(const_loaded, 16)
                col += width
            act.dma_start(masks[:], level_masks).then_inc(const_loaded, 16)
            act.dma_start(bif[:], b_if).then_inc(const_loaded, 16)
            act.dma_start(m0t[:], m0).then_inc(const_loaded, 16)
            act.wait_ge(init_done, 1)
            act.wait_ge(const_loaded, 16 * CONST_LOADS)

            def ln_1p_exp_neg_abs(dst, src, done):
                chain.link(act.activation(dst, src, ACT.Abs))
                chain.link(act.activation(dst, dst, ACT.Exp, scale=-1.0))
                act.activation(dst, dst, ACT.Ln, bias=one_t[0:dst.shape[0], :]).then_inc(done, 1)

            for l in range(DEPTH):
                ln_1p_exp_neg_abs(c8[:, l * KT:(l + 1) * KT],
                                  V[:, l * V_COLS + V_LAM:l * V_COLS + V_LAM + KT], c8_in)

            act.wait_ge(x_loaded, 16)
            for m in range(KT):
                if m:
                    act.wait_ge(acc_ready, m)
                act.activation(sq[:], x[:, m, :], ACT.Square).then_inc(sq_ready, 1)

            def norm_root(k, tokens_too=False):
                act.wait_ge(norm_sum, k + 1)
                if tokens_too:
                    act.activation(sdT[:], Q[:, 2, 0:NC + 1], ACT.Sqrt, bias=eps_t[:], scale=1.0 / D)
                act.activation(halves(sd[:]), banks(Q[:, 0:2]), ACT.Sqrt, bias=eps_t[:],
                               scale=1.0 / D).then_inc(sd_ready, 1)

            def tile_taken(t):
                act.wait_ge(tile_free, t + 3)

            def squares(t, m):
                tile_taken(t)
                act.activation(sq[:], x[:, m, :], ACT.Square).then_inc(sq_ready, 1)

            def ffn(L, first_tile, norm):
                t = L * LAYER_TILES + first_tile
                norm_root(norm)
                for half, tiles in enumerate(FF_HALVES):
                    with act.Fori(0, tiles // 2) as i:
                        for j in range(2):
                            tile_taken(i * 4 + (t + 2 * j))
                            act.activation(sg[:], gs[:], ACT.Silu).then_inc(silu_done, 1)
                    t = t + 2 * tiles
                    if half == 1:
                        with act.Fori(0, KT // 2) as i:
                            for j in range(2):
                                squares(i * 2 + (t + j), i * 2 + j)
                    t = t + KT

            def gate_tiles(t):
                for v in range(2):
                    tile_taken(t + v)
                    act.activation(Gm[:, v, :], tg[:], ACT.Sigmoid).then_inc(gate_act, 1)
                for v in range(2):
                    yield
                    tile_taken(t + 2 + v)
                    act.activation(tg[:], tg[:], ACT.Sigmoid).then_inc(gate_act, 1)

            def head_root():
                act.activation(halves(hsq[:, 1, :]), banks(Q[:, 0:2]), ACT.Sqrt, bias=eps_t[:],
                               scale=1.0 / DV).then_inc(root_done, 1)

            def mlstm_head(L, i):
                B = L * HEADS + i
                t = L * LAYER_TILES + i * HEAD_TILES + (TILE_MIX + GATE_TILES)
                stored = L * (16 * STORES) + i * 48 + 32
                act.wait_ge(rows_stored, L * 16 + 16)
                act.dma_start(RB.rearrange("p a b -> p (a b)"),
                              spread(rows_dram[ds(i, 1), :], 0, P)).then_inc(a_rows, 16)
                act.wait_ge(a_rows, B * 16 + 16)
                act.activation(SI, RB[:, 1, :], ACT.Exp)
                act.activation(EM, RB[:, 2, :], ACT.Exp).then_inc(a_si, 1)
                act.wait_ge(state_stored, stored)
                act.dma_start(CS[:], c0[L, i]).then_inc(a_cs, 16)
                act.dma_start(nS[:, 0, :], n0[L, i]).then_inc(a_cs, 16)
                act.wait_ge(a_exin, B + 1)
                for c in range(NC):
                    sl = slice(c * C, (c + 1) * C)
                    act.activation(Ex[:, sl], Ex[:, sl], ACT.Exp, bias=cols[:, c:c + 1])
                act.activation(Ex[0:NS, T:N], Ex[0:NS, T:N], ACT.Exp, bias=cols[0:NS, NC:NC + 1]).then_inc(a_ex, 1)
                gates = gate_tiles(t + 4)
                next(gates)
                act.wait_ge(a_c, B * NC + NC)
                act.dma_start(o_pc[L, i], Cst[:, NC - 1, 0:DV + 1]).then_inc(state_stored, 16)
                next(gates)
                act.wait_ge(a_hc, B + 1)
                act.activation(hsq[:], Hh[:], ACT.Square).then_inc(a_sq, 1)
                next(gates, None)
                act.wait_ge(a_var, B + 1)
                head_root()
                act.wait_ge(head_samples, L * (4 * HEADS) + i * 2 + 3)
                act.dma_start(o_sc[L, i], CS[:]).then_inc(state_stored, 16)
                act.dma_start(o_sn[L, i], nS[:, 1, :]).then_inc(state_stored, 16)

            def gla_head(L, i, last=False):
                B = L * HEADS + i
                t = L * LAYER_TILES + i * HEAD_TILES + (TILE_MIX + GATE_TILES + HEADS * HEAD_TILES)
                stored = L * (16 * STORES) + i * 32 + (32 + 48 * HEADS)
                chain.restart()
                act.wait_ge(b_zin, B + 1)
                if not last:
                    act.dma_start(lr2[64:80, :], w_lr2[L, i + 1]).then_inc(b_lr, 16)
                ln_1p_exp_neg_abs(seven[:, 1, :], seven[:, 0, :], b_ln)
                act.wait_ge(state_stored, stored)
                act.dma_start(CS[:], s0[L, i]).then_inc(b_cs, 16)
                act.wait_ge(b_diff, B + 1)
                inv = 1.0 / 16.0
                act.activation(seven[:, 0:NL - NLS, 0:T], seven[:, 0:NL - NLS, 0:T], ACT.Exp, scale=inv)
                act.activation(seven[:, NL - NLS:NL, :], seven[:, NL - NLS:NL, :], ACT.Exp, scale=inv)
                act.activation(eb[:], bc[:], ACT.Exp, scale=inv)
                act.activation(kh[:], kh[:], ACT.Exp, scale=inv).then_inc(b_exp, 1)
                gates = gate_tiles(t + 4)
                next(gates)
                act.wait_ge(b_c, B * NC + NC)
                act.dma_start(o_ps[L, i], Cst[:, NC - 1, 0:DV]).then_inc(state_stored, 16)
                next(gates)
                act.wait_ge(b_h, B + 1)
                act.activation(hsq[:], Hh[:], ACT.Square).then_inc(b_sq, 1)
                next(gates, None)
                act.wait_ge(b_var, B + 1)
                head_root()
                act.wait_ge(head_samples, L * (4 * HEADS) + i * 2 + (2 * HEADS + 3))
                act.dma_start(o_ss[L, i], CS[:]).then_inc(state_stored, 16)

            def lru_pair(L, i, j2):
                pr = L * (KT // 2) + i * 2 + j2
                t = L * LAYER_TILES + i * 12 + (TILE_MIX + GATE_TILES + 2 * HEADS * HEAD_TILES + 6 * j2)

                def gates(j):
                    k = pr * 2 + j
                    g = L * V_COLS + i * 4 + (2 * j2 + j)
                    act.wait_ge(l_ri, k + 1)
                    act.activation(halves(rr[:]), banks(Q[:, 0:2]), ACT.Sigmoid, bias=V[:, ds(g + V_BA, 1)])
                    act.activation(halves(ii[:]), banks(Q[:, 2:4]), ACT.Sigmoid,
                                   bias=V[:, ds(g + V_BI, 1)]).then_inc(l_sig, 1)
                    act.wait_ge(l_sig, k + 2)
                    c = L * KT + i * 4 + (2 * j2 + j)
                    act.activation(aa[:], rr[:], ACT.Exp, scale=c8[:, ds(c, 1)])
                    act.activation(tt[:], rr[:], ACT.Tanh, scale=nc8[:, ds(c, 1)]).then_inc(l_at, 1)
                    act.wait_ge(l_min, k + 1)
                    act.activation(tt[:], tt[:], ACT.Sqrt).then_inc(l_mult, 1)

                def gelu(v):
                    tile_taken(t + 2 + v)
                    act.activation(lyg[:, v, :], lyg[:, v, :], ACT.Gelu_apprx_tanh).then_inc(l_act, 1)

                gates(0)
                gelu(0)
                gates(1)
                gelu(1)
                for v in range(2):
                    tile_taken(t + 4 + v)
                    act.activation(tt[:], tt[:], ACT.Sigmoid).then_inc(l_act, 1)

            with act.Fori(0, DEPTH) as L:
                ffn(L, 0, L * 3)
                norm_root(L * 3 + 1, tokens_too=True)
                chain.restart()
                act.wait_ge(gate_in, L + 1)
                ln_1p_exp_neg_abs(merged[0:HEADS, 6, :], merged[0:HEADS, 5, :], gate_ln)
                act.wait_ge(rows_ready, L + 1)
                act.dma_start(rows_dram, merged[0:HEADS, 0:4, :].rearrange("h a b -> h (a b)")).then_inc(rows_stored, 16)
                act.dma_start(o_pm[L], m_out[:, 0:1]).then_inc(state_stored, 16)
                act.dma_start(o_sm[L], m_out[:, 1:]).then_inc(state_stored, 16)
                with act.Fori(0, HEADS) as i:
                    mlstm_head(L, i)
                act.dma_start(lr2[64:80, :], w_lr2[L, 0]).then_inc(b_lr, 16)
                with act.Fori(0, HEADS - 1) as i:
                    gla_head(L, i)
                gla_head(L, HEADS - 1, last=True)
                act.wait_ge(heads_done, L + 1)
                act.wait_ge(state_stored, L * (16 * STORES) + 16 * (STORES - 4))
                act.dma_start(h0t[:], h0[L]).then_inc(l_vec, 16)
                act.dma_start(cv0[:], conv0[L]).then_inc(l_vec, 16)
                with act.Fori(0, KT // 4) as i:
                    act.dma_start(wra[:], w_ra[L, i]).then_inc(l_w, 16)
                    act.dma_start(wri[:], w_ri[L, i]).then_inc(l_w, 16)
                    lru_pair(L, i, 0)
                    lru_pair(L, i, 1)
                act.wait_ge(lru_done, L * (KT // 2) + KT // 2 + 1)
                for dst, src in ((o_ph[L], ph), (o_sh[L], sh), (o_pconv[L], pcv), (o_sconv[L], scv)):
                    act.dma_start(dst, src[:]).then_inc(state_stored, 16)
                with act.Fori(0, KT // 2) as i:
                    for j in range(2):
                        squares(L * LAYER_TILES + i * 2 + (TILE_OUT + j), i * 2 + j)
                ffn(L, TILE_FFN2, L * 3 + 2)
            chain.end()
            norm_root(3 * DEPTH)

        @block.vector
        def _(dve):
            chain = Chain(dve, dve_chain, init_done)
            link = chain.link
            tt_, ts_, stt = dve.tensor_tensor, dve.tensor_scalar, dve.scalar_tensor_tensor
            rs2 = halves(rstd[:])

            def tile_ready(t):
                dve.wait_ge(tile_done, t + 3)

            def take(t, slot, dst, scale=None):
                tile_ready(t)
                if scale is None:
                    ins = tt_(halves(dst), banks(pair[slot]), rs2, ALU.mult)
                else:
                    ins = stt(halves(dst), banks(pair[slot]), scale, rs2, ALU.mult, ALU.mult)
                ins.then_inc(tile_free, 1)
                dve.wait_ge(tile_free, t + 3)

            def prepare(m, g_col, n_sq):
                link(ts_(xg[:], x[:, m, :], V[:, ds(g_col, 1)], None, ALU.mult))
                link(dve.tensor_copy(xh[:, m, :], xg[:]))
                tt_(xl[:, m, :], xg[:], xh[:, m, :].bitcast(F32), ALU.subtract)
                dve.wait_ge(sq_ready, n_sq + 1)
                tt_(acc[:], acc[:], sq[:], ALU.add).then_inc(acc_ready, 1)
                dve.wait_ge(acc_ready, n_sq + 1)

            def residual(t, slot, m, scale):
                tile_ready(t)
                stt(halves(x[:, m, :]), banks(pair[slot]), scale, halves(x[:, m, :]),
                    ALU.mult, ALU.add).then_inc(tile_free, 1)
                dve.wait_ge(tile_free, t + 3)

            def clear_acc():
                chain.restart()
                link(dve.memset(acc[:], 0.0))

            def reciprocal_norm(k):
                dve.wait_ge(sd_ready, k + 1)
                chain.restart()
                link(dve.reciprocal(rstd[:], sd[:]))

            def ffn(L, first_tile, h_base, norm, g_col):
                t = L * LAYER_TILES + first_tile
                hd = L * (2 * sum(FF_HALVES)) + h_base
                reciprocal_norm(norm)
                for half, tiles in enumerate(FF_HALVES):
                    with dve.Fori(0, tiles // 2) as i:
                        chain.restart()
                        for j in range(2):
                            tj = i * 4 + (t + 2 * j)
                            take(tj, 0, gs[:])
                            take(tj + 1, 1, us[:])
                            dve.wait_ge(silu_done, hd + i * 2 + (j + 1))
                            link(tt_(hp[:], sg[:], us[:], ALU.mult))
                            hi = hh[:, i * 2 + j, :]
                            link(dve.tensor_copy(hi, hp[:]))
                            tt_(hl[:, i * 2 + j, :], hp[:], hi.bitcast(F32), ALU.subtract).then_inc(h_done, 1)
                            dve.wait_ge(h_done, hd + i * 2 + (j + 1))
                    t, hd = t + 2 * tiles, hd + tiles
                    if half == 1:
                        clear_acc()
                    with dve.Fori(0, KT // 2) as i:
                        chain.restart()
                        for j in range(2):
                            residual(i * 2 + (t + j), j, i * 2 + j, 0.5)
                            if half == 1:
                                prepare(i * 2 + j, g_col + i * 2 + j, norm * KT + i * 2 + (KT + j))
                    t = t + KT

            dve.wait_ge(const_loaded, 16 * CONST_LOADS)
            dve.wait_ge(c8_in, DEPTH)
            for l in range(DEPTH):
                s_ = slice(l * KT, (l + 1) * KT)
                lam = V[:, l * V_COLS + V_LAM:l * V_COLS + V_LAM + KT]
                link(ts_(t8[:, 0:KT], lam, -1.0, 0.0, ALU.mult, ALU.max))
                link(tt_(t8[:, 0:KT], t8[:, 0:KT], c8[:, s_], ALU.add))
                link(ts_(c8[:, s_], t8[:, 0:KT], -8.0, None, ALU.mult))
                link(ts_(nc8[:, s_], t8[:, 0:KT], 8.0, None, ALU.mult))
            dve.memset(t8[:], 0.0).then_inc(tile_free, 2)
            dve.wait_ge(tile_free, 2)
            dve.memset(t8[:], 0.0).then_inc(root_done, 1)
            dve.wait_ge(root_done, 1)
            dve.memset(t8[:], 0.0).then_inc(head_samples, 1)
            dve.wait_ge(head_samples, 1)
            dve.memset(t8[:], 0.0).then_inc(l_sig, 1)
            dve.wait_ge(l_sig, 1)
            dve.memset(t8[:], 0.0).then_inc(lru_done, 1)
            dve.wait_ge(lru_done, 1)
            dve.wait_ge(x_loaded, 16)
            clear_acc()
            for m in range(KT):
                prepare(m, V_FIRST + m, m)

            def gate_rows(L):
                R = [merged[0:HEADS, r, :] for r in range(KT)]
                tile_ready(L * LAYER_TILES + (TILE_MIX + 1))
                g = banks(pair[0])
                link(tt_(halves(R[4]), g[0:HEADS], rs2[0:HEADS], ALU.mult))
                link(tt_(halves(R[5]), g[32:32 + HEADS], rs2[32:32 + HEADS], ALU.mult))
                tt_(halves(glr), g[64:80], rs2[64:80], ALU.mult).then_inc(tile_free, GATE_TILES)
                link(ts_(R[4], R[4], bif[:, ds(L, 1), 0], None, ALU.add))
                ts_(R[5], R[5], bif[:, ds(L, 1), 1], None, ALU.add).then_inc(gate_in, 1)
                dve.wait_ge(gate_ln, L + 1)
                link(stt(R[7], R[5], 0.0, R[6], ALU.min, ALU.subtract))
                link(dve.tensor_tensor_scan(R[5], reset[0:HEADS, :], R[7], 0.0, ALU.mult, ALU.add))
                link(tt_(R[3], R[4], R[5], ALU.subtract))
                m0_ = m0t[:, ds(L, 1), :].rearrange("p a s -> p (a s)")
                link(tt_(t8[0:HEADS, :], R[7][:, T:N:TS], m0_, ALU.add))
                link(dve.tensor_copy(R[6], R[7]))
                link(dve.memset(R[6][:, T:N:TS], NEG))
                link(dve.tensor_copy(R[0], R[4]))
                link(tt_(R[0][:, T:N:TS], R[4][:, T:N:TS], t8[0:HEADS, :], ALU.max))
                link(dve.tensor_tensor_scan(R[7], R[6], R[0], 0.0, ALU.add, ALU.max))
                link(ts_(R[2], R[7], -1.0, None, ALU.mult))
                link(tt_(R[0], R[5], R[7], ALU.subtract))
                link(dve.tensor_copy(R[1][:, 0:C], R[0][:, 0:C]))
                for c in range(1, NC):
                    link(ts_(R[1][:, c * C:(c + 1) * C], R[0][:, c * C:(c + 1) * C], R[7][:, c * C - 1:c * C],
                             None, ALU.add))
                sv = [r[:, T:N].rearrange("p (s t) -> p s t", t=TS) for r in R]
                link(tt_(sv[1], sv[0], spread(m0_.unsqueeze(2), 2, TS), ALU.add))
                link(dve.tensor_copy(m_out[:, 0:1], R[7][:, T - 1:T]))
                dve.tensor_copy(m_out[:, 1:], R[7][:, T + TS - 1:N:TS]).then_inc(rows_ready, 1)

            def take_values(t):
                take_prompt_values(t)
                take_sample_values(t + 1)

            def take_prompt_values(t):
                tile_ready(t)
                tt_(val[:, 0:NC, 0:DV], pair[0][:].rearrange("p a (b v) -> p (a b) v", b=2),
                    spread(rstdT[:, 0:NC].unsqueeze(2), 2, DV), ALU.mult).then_inc(tile_free, 1)
                dve.wait_ge(tile_free, t + 3)

            def take_sample_values(t):
                tile_ready(t)
                ts_(val[0:NS, NC, 0:DV], pair[1][C - NS:C, 0, 0:DV], rstdT[C - NS:C, NC:NC + 1], None,
                    ALU.mult).then_inc(tile_free, 1)
                dve.wait_ge(tile_free, t + 3)

            def take_gate(L, i, t, slot, v, acts, kind, g_col):
                take(t, slot, tg[:])
                dve.wait_ge(gate_act, acts + 1)
                if kind == "silu":
                    link(tt_(Gm[:, v, :], Gm[:, v, :], tg[:], ALU.mult))
                if kind == "branch":
                    link(stt(Gm[:, v, :], Gm[:, v, :], V[:, ds(g_col, 1)], tg[:], ALU.mult, ALU.mult))

            def states(c_, width, dec, b_of, up, done, base):
                dve.wait_ge(up, base + (c_ + 1))
                src = Q[:, b_of(c_), 0:width]
                if c_ == 0:
                    ins = dve.tensor_copy(Cst[:, 0, 0:width], src)
                else:
                    ins = stt(Cst[:, c_, 0:width], Cst[:, c_ - 1, 0:width], dec(c_), src, ALU.mult, ALU.add)
                ins.then_inc(done, 1)
                dve.wait_ge(done, base + (c_ + 1))

            def sample_states(decay, half, updated, k_up, number):
                dve.wait_ge(updated, k_up + 1)
                for e in range(SEQS // 2):
                    s_ = half * SEQS // 2 + e
                    k = T + s_ * TS + TS - 1
                    ins = stt(CS[:, s_, :], CS[:, s_, :], decay[:, k:k + 1],
                              Q[:, 2 + e // 2, e % 2 * DV:(e % 2 + 1) * DV], ALU.mult, ALU.add)
                ins.then_inc(head_samples, 1)
                dve.wait_ge(head_samples, number + 2)

            def square_sum(squared, k, done):
                dve.wait_ge(squared, k + 1)
                tt_(hsq[:, 0, :], hsq[:, 0, :], hsq[:, 1, :], ALU.add).then_inc(done, 1)
                dve.wait_ge(done, k + 1)

            def merge_head(i, first, number, done=None):
                dve.wait_ge(root_done, number + 2)
                link(dve.reciprocal(hsq[:, 1, :], hsq[:, 1, :]))
                r = spread(hsq[:, 1, :].unsqueeze(1), 1, 2)
                mo_ = merged[:, ds(i * 2, 2), :]
                if first:
                    link(tt_(mo_, Hh[:], r, ALU.mult))
                else:
                    link(tt_(Hh[:], Hh[:], r, ALU.mult))
                    ins = tt_(mo_, mo_, Hh[:], ALU.add)
                    if done is None:
                        link(ins)
                    else:
                        ins.then_inc(done, 1)

            def mlstm_head(L, i, first=False):
                B = L * HEADS + i
                number = L * (2 * HEADS) + i
                t = L * LAYER_TILES + i * HEAD_TILES + (TILE_MIX + GATE_TILES)
                acts = L * (8 * HEADS) + i * 4
                gcol = L * V_COLS + i * 2 + V_GML
                chain.restart()
                take(t, 0, qT[:])
                take(t + 1, 1, kT[:], DK ** -0.5)
                dve.wait_ge(a_si, B + 1)
                link(tt_(qs[:], qT[:], SI, ALU.mult))
                take_values(t + 2)
                link(tt_(Ex[:, 0:T].rearrange("p (c t) -> p c t", c=NC),
                         RB[:, 0, 0:T].rearrange("p (c t) -> p c t", c=NC),
                         spread(neg_p[:].unsqueeze(1), 1, NC), ALU.add))
                link(tt_(Ex[0:NS, T:N], RB[0:NS, 0, T:N], neg_s[:], ALU.add))
                dve.wait_ge(a_scores, B + 1)
                link(dve.tensor_copy(cols[0:NS, NC:NC + 1], Q[0:NS, 2, 200 + NC:201 + NC]))
                dve.tensor_copy(cols[:, 0:NC], Q[:, 2, 200:200 + NC]).then_inc(a_exin, 1)
                dve.wait_ge(a_ex, B + 1)
                exv = Ex[:, 0:T].rearrange("p (c t) -> p c t", c=NC)
                link(tt_(wS[:, 0:T], Ex[:, 0:T], Q[:, 0, :], ALU.mult))
                link(tt_(wS[0:NS, T:N], Ex[0:NS, T:N], Q[0:NS, 2, 0:NS], ALU.mult))
                link(tt_(Kw[:], Q[:, 1, :].rearrange("p (c t) -> p c t", c=NC),
                         spread(exv[:, :, C - 1:C], 2, P), ALU.mult))
                link(dve.tensor_copy(Kts[:], Q[0:NS, 2, NS:NS + P]))
                tt_(Kws[:], spread(Kts[:].unsqueeze(1), 1, SEQS),
                    spread(Ex[0:NS, T + TS - 1:N:TS].unsqueeze(2), 2, P), ALU.mult).then_inc(a_kw, 1)

                if not first:
                    merge_head(i - 1, True, number - 1)
                dve.wait_ge(a_cs, B * 32 + 32)
                link(tt_(qn[:].rearrange("p (s t) -> p s t", t=TS), qs[:, T:N].rearrange("p (s t) -> p s t", t=TS),
                         spread(nS[:, 0, :].unsqueeze(2), 2, TS), ALU.mult))
                take_gate(L, i, t + 4, 0, 0, acts, "sigmoid", None)
                for c in range(NC):
                    states(c, DV + P, lambda c: SI[:, c * C + C - 1:(c + 1) * C], lambda c: c, a_u, a_c, B * NC)
                take_gate(L, i, t + 5, 1, 1, acts + 1, "sigmoid", None)
                dve.wait_ge(a_den, B + 1)
                for sl, den in ((slice(0, T), Q[:, 2, :]), (slice(T, N), Q[:, 3, 2 * NS:3 * NS])):
                    link(stt(tg[:, sl], den, -1.0, EM[:, sl], ALU.mult, ALU.max))
                    link(tt_(tg[:, sl], tg[:, sl], den, ALU.max))
                link(dve.reciprocal(tg[:], tg[:]))
                link(tt_(nS[:, 1, :], nS[:, 0, :], SI[:, T + TS - 1:N:TS], ALU.mult))
                link(tt_(Hh[:, :, T:N], Q[:, 3, 0:2 * NS].rearrange("p (v t) -> p v t", v=2),
                         spread(tg[:, T:N].unsqueeze(1), 1, 2), ALU.mult))
                link(tt_(nS[:, 1, :], nS[:, 1, :], Q[:, 3, 3 * NS:3 * NS + SEQS], ALU.add))
                dve.wait_ge(a_out, B + 1)
                link(tt_(Hh[:, :, 0:T], Q[:, 0:2, :], spread(tg[:, 0:T].unsqueeze(1), 1, 2), ALU.mult))
                tt_(wS[:], Hh[:, 0, :], Hh[:, 1, :], ALU.add).then_inc(a_h, 1)
                take_gate(L, i, t + 6, 0, 0, acts + 2, "branch", gcol)
                dve.wait_ge(a_mean, B + 1)
                for v in range(2):
                    ins = stt(halves(Hh[:, v, :]), banks(Q[:, 0:2]), -1.0 / DV, halves(Hh[:, v, :]), ALU.mult, ALU.add)
                ins.then_inc(a_hc, 1)
                sample_states(SI, 0, a_us, B * 2, number * 2)
                square_sum(a_sq, B, a_sqs)
                take_gate(L, i, t + 7, 1, 1, acts + 3, "branch", gcol + 1)
                link(tt_(Hh[:], Hh[:], Gm[:], ALU.mult))
                sample_states(SI, 1, a_us, B * 2 + 1, number * 2 + 1)

            def gla_head(L, i, first=False):
                B = L * HEADS + i
                number = L * (2 * HEADS) + i + HEADS
                t = L * LAYER_TILES + i * HEAD_TILES + (TILE_MIX + GATE_TILES + HEADS * HEAD_TILES)
                acts = L * (8 * HEADS) + i * 4 + 4 * HEADS
                gcol = L * V_COLS + i * 2 + V_GGLA
                chain.restart()
                dve.wait_ge(b_z, B + 1)
                z, l_, la = seven[:, 0, :], seven[:, 1, :], seven[:, 2, :]
                ts_(halves(z), banks(Q[:, 0:2]), V[:, ds(L * V_COLS + i + V_BGLA, 1)], None,
                    ALU.add).then_inc(b_zin, 1)
                dve.wait_ge(b_ln, B + 1)
                link(stt(la, z, 0.0, l_, ALU.min, ALU.subtract))
                link(dve.tensor_tensor_scan(bc[:], reset[:], la, 0.0, ALU.mult, ALU.add))
                for l in range(NL):
                    h_ = LEVELS[l]
                    m_ = N if l >= NL - NLS else T
                    bv = bc[:, 0:m_].rearrange("p (n a h) -> p n a h", a=2, h=h_)
                    ev = seven[:, l, 0:m_].rearrange("p (n a h) -> p n a h", a=2, h=h_)
                    mid = spread(bv[:, :, 0, h_ - 1:h_], 2, h_)
                    tt_(ev[:, :, 1, :], bv[:, :, 1, :], mid, ALU.subtract)
                    ins = tt_(ev[:, :, 0, :], mid, bv[:, :, 0, :], ALU.subtract)
                link(ins)
                bp = bc[:, 0:T].rearrange("p (c t) -> p c t", c=NC)
                bs = bc[:, T:N].rearrange("p (c t) -> p c t", c=SEQS)
                tt_(kh[:, 0:T].rearrange("p (c t) -> p c t", c=NC), spread(bp[:, :, C - 1:C], 2, C), bp, ALU.subtract)
                tt_(kh[:, T:N].rearrange("p (c t) -> p c t", c=SEQS), spread(bs[:, :, TS - 1:TS], 2, TS), bs,
                    ALU.subtract).then_inc(b_diff, 1)
                take(t, 0, qT[:], DK ** -0.5)
                take(t + 1, 1, kT[:])
                dve.wait_ge(b_exp, B + 1)
                for l in range(NL):
                    if l == NL // 2:
                        take_prompt_values(t + 2)
                    h_ = LEVELS[l]
                    m_ = N if l >= NL - NLS else T
                    ev = seven[:, l, 0:m_].rearrange("p (n a h) -> p n a h", a=2, h=h_)
                    for a, src in ((1, qT), (0, kT)):
                        sv = src[:, 0:m_].rearrange("p (n a h) -> p n a h", a=2, h=h_)
                        tt_(ev[:, :, a, :], ev[:, :, a, :], sv[:, :, a, :], ALU.mult)
                tt_(qs[:], qT[:], eb[:], ALU.mult)
                link(tt_(kh[:], kh[:], kT[:], ALU.mult))
                take_sample_values(t + 3)
                dve.memset(t8[:], 0.0).then_inc(b_fac, 1)
                take_gate(L, i, t + 4, 0, 0, acts, "silu", None)

                def ring(r):
                    dve.wait_ge(b_ring, B * 10 + (r + 1))

                def level(r):
                    ring(r)
                    av = wS[:, 0:T].rearrange("p (c t) -> p c t", c=NC)
                    src = Q[:, r % 4, :].rearrange("p (c t) -> p c t", c=NC)
                    if r == 0:
                        ins = tt_(av, src, spread(ident[:].unsqueeze(1), 1, NC), ALU.mult)
                    else:
                        chain.hold()
                        ins = dve.copy_predicated(av, spread(masks[:, r - 1, :].unsqueeze(1), 1, NC), src)
                    ins.then_inc(b_took, 1)
                    dve.wait_ge(b_took, B * 10 + (r + 1))

                for r in range(NL + 1):
                    level(r)
                ring(8)
                dve.tensor_copy(Kw[:], Q[:, 0, :].rearrange("p (c t) -> p c t", c=NC)).then_inc(b_took, 1)
                ring(9)
                As = wS[0:NS, T:N]
                link(tt_(As, Q[0:NS, 1, 0:NS], ident[0:NS, 0:NS], ALU.mult))
                for e in range(NLS):
                    link(dve.copy_predicated(As, masks[0:NS, NL - NLS + e, 0:NS], Q[0:NS, 1, (e + 1) * NS:(e + 2) * NS]))
                tt_(Kws[:], spread(Q[0:NS, 1, P:2 * P].unsqueeze(1), 1, SEQS),
                    spread(seqm[:].unsqueeze(2), 2, P), ALU.mult).then_inc(b_took, 1)
                take_gate(L, i, t + 5, 1, 1, acts + 1, "silu", None)
                for c in range(NC):
                    states(c, DV, lambda c_: eb[:, c_ * C + C - 1:(c_ + 1) * C], lambda c_: c_, b_u, b_c, B * NC)
                merge_head(HEADS - 1 if first else i - 1, first, number - 1)
                take_gate(L, i, t + 6, 0, 0, acts + 2, "branch", gcol)
                dve.wait_ge(b_out, B + 1)
                dve.tensor_copy(Hh[:, :, 0:T], Q[:, 0:2, :])
                dve.tensor_copy(Hh[:, :, T:N], Q[:, 2, 0:2 * NS].rearrange("p (v t) -> p v t", v=2)).then_inc(b_h, 1)
                square_sum(b_sq, B, b_sqs)
                take_gate(L, i, t + 7, 1, 1, acts + 3, "branch", gcol + 1)
                link(tt_(Hh[:], Hh[:], Gm[:], ALU.mult))
                sample_states(eb, 0, b_us, B * 2, number * 2)
                sample_states(eb, 1, b_us, B * 2 + 1, number * 2 + 1)

            def lru_pair(L, i, j2):
                pr = L * (KT // 2) + i * 2 + j2
                t = L * LAYER_TILES + i * 12 + (TILE_MIX + GATE_TILES + 2 * HEADS * HEAD_TILES + 6 * j2)
                chain.restart()

                def at(j):
                    return i * 4 + (2 * j2 + j)

                def take_x(j):
                    tile_ready(t + j)
                    tt_(lxp[:, j, 3:3 + HALF], pair[j][:, 0, 0:HALF], rstd[:, 0:HALF], ALU.mult)
                    tt_(lxp[:, j, 3 + HALF:3 + T], pair[j][:, 1, 0:T - HALF], rstd[:, HALF:T], ALU.mult)
                    dve.tensor_copy(lxs[:, j, :, 0:3], cv0[:, at(j), :, :])
                    tt_(lxs[:, j, :, 3:3 + TS],
                        pair[j][:, 1, T - HALF:HALF].rearrange("p (s t) -> p s t", t=TS),
                        rstd[:, T:N].rearrange("p (s t) -> p s t", t=TS), ALU.mult).then_inc(tile_free, 1)
                    dve.wait_ge(tile_free, t + (j + 3))

                def conv(j):
                    col = L * V_COLS + i * 4 + (2 * j2 + j)
                    xs = xc[:, j, T:N].rearrange("p (s t) -> p s t", t=TS)
                    w = [V[:, ds(col + (V_CONV + KT * a), 1)] for a in range(4)]
                    b = V[:, ds(col + V_BCONV, 1)]
                    ts_(xc[:, j, 0:T], lxp[:, j, 0:T], w[0], b, ALU.mult, ALU.add)
                    link(ts_(xs, lxs[:, j, :, 0:TS], w[0], b, ALU.mult, ALU.add))
                    for a in range(1, 4):
                        stt(xc[:, j, 0:T], lxp[:, j, a:a + T], w[a], xc[:, j, 0:T], ALU.mult, ALU.add)
                        ins = stt(xs, lxs[:, j, :, a:a + TS], w[a], xs, ALU.mult, ALU.add)
                        if a < 3:
                            link(ins)
                    ins.then_inc(l_xc, 1)
                    dve.tensor_copy(pcv[:, at(j), :], lxp[:, j, T:T + 3])
                    dve.tensor_copy(scv[:, at(j), :, :], lxs[:, j, :, TS:TS + 3])

                def recur(j):
                    k = pr * 2 + j
                    dve.wait_ge(l_at, k + 1)
                    link(tt_(hseq[:, j, :], aa[:], aa[:], ALU.mult))
                    stt(tt[:], hseq[:, j, :], 1.0, tt[:], ALU.add, ALU.mult).then_inc(l_min, 1)
                    link(tt_(ii[:], ii[:], xc[:, j, :], ALU.mult))
                    dve.wait_ge(l_mult, k + 1)
                    link(dve.memset(tt[:, 0:1], 1.0))
                    link(tt_(ii[:], ii[:], tt[:], ALU.mult))
                    starts = slice(T, N, TS)
                    link(tt_(t8[:], aa[:, starts], h0t[:, at(j), :], ALU.mult))
                    link(tt_(ii[:, starts], ii[:, starts], t8[:], ALU.add))
                    link(dve.memset(aa[:, starts], 0.0))
                    link(dve.tensor_tensor_scan(hseq[:, j, :], aa[:], ii[:], 0.0, ALU.mult, ALU.add))
                    dve.tensor_copy(ph[:, ds(at(j), 1)], hseq[:, j, T - 1:T])
                    link(dve.tensor_copy(sh[:, at(j), :], hseq[:, j, T + TS - 1:N:TS]))

                def take_y(v):
                    take(t + 2 + v, v, lyg[:, v, :])

                take_x(0)
                conv(0)
                take_x(1)
                conv(1)
                recur(0)
                take_y(0)
                recur(1)
                take_y(1)
                for v in range(2):
                    take(t + 4 + v, v, tt[:])
                    dve.wait_ge(l_act, pr * 4 + (3 + v))
                    link(tt_(tt[:], tt[:], lyg[:, v, :], ALU.mult))
                    link(tt_(tt[:], tt[:], hseq[:, v, :], ALU.mult))
                    link(tt_(tt[:], tt[:], merged[:, at(v), :], ALU.add))
                    link(dve.tensor_copy(mh[:, at(v), :], tt[:]))
                    tt_(ml[:, at(v), :], tt[:], mh[:, at(v), :].bitcast(F32), ALU.subtract).then_inc(m_ready, 1)
                    dve.wait_ge(m_ready, pr * 2 + (v + 1))
                dve.memset(t8[:], 0.0).then_inc(lru_done, 1)
                dve.wait_ge(lru_done, pr + 2)

            with dve.Fori(0, DEPTH) as L:
                ffn(L, 0, 0, L * 3, L * V_COLS + V_MIX)
                reciprocal_norm(L * 3 + 1)
                link(dve.reciprocal(rstdT[:], sdT[:]))
                gate_rows(L)
                dve.wait_ge(rows_ready, L + 1)
                chain.restart()
                link(dve.memset(val[:, :, DV:DV + P], 1.0))
                mlstm_head(L, 0, first=True)
                chain.hold()
                with dve.Fori(1, HEADS) as i:
                    mlstm_head(L, i)
                gla_head(L, 0, first=True)
                chain.hold()
                with dve.Fori(1, HEADS) as i:
                    gla_head(L, i)
                chain.restart()
                merge_head(HEADS - 1, False, L * (2 * HEADS) + (2 * HEADS - 1), heads_done)
                dve.wait_ge(heads_done, L + 1)
                dve.wait_ge(l_vec, L * 32 + 32)
                link(dve.memset(lxp[:, :, 0:3], 0.0))
                with dve.Fori(0, KT // 4) as i:
                    lru_pair(L, i, 0)
                    lru_pair(L, i, 1)
                clear_acc()
                with dve.Fori(0, KT // 2) as i:
                    chain.restart()
                    for j in range(2):
                        residual(L * LAYER_TILES + i * 2 + (TILE_OUT + j), j, i * 2 + j, 1.0)
                        prepare(i * 2 + j, L * V_COLS + i * 2 + (V_FFN2 + j), L * (3 * KT) + i * 2 + (2 * KT + j))
                dve.wait_ge(state_stored, L * (16 * STORES) + 16 * STORES)
                ffn(L, TILE_FFN2, sum(FF_HALVES), L * 3 + 2, L * V_COLS + V_NEXT)
            reciprocal_norm(3 * DEPTH)
            chain.end()
            for m in range(KT):
                g = (DEPTH - 1) * V_COLS + V_NEXT + m
                stt(x[:, m, :], x[:, m, :], V[:, g:g + 1], rstd[:], ALU.mult, ALU.mult).then_inc(y_ready, 1)


def _layout(inputs):
    import numpy as np

    a = {k: np.asarray(v) for k, v in inputs.items()}
    f = np.float32
    out = {}
    xs = np.concatenate([a["x_prompt"][0], a["x_sample"].reshape(NS, D)])
    out["x_T"] = xs.T.reshape(KT, P, N).transpose(1, 0, 2)

    def up(w):
        w = w.reshape(DEPTH, KT, P, 2, FF // P, P)
        return w.transpose(0, 4, 2, 1, 3, 5).reshape(DEPTH, FF // P, P, 2 * D)

    def down(w):
        w = w.reshape(DEPTH, FF // P, P, KT, P).transpose(0, 3, 2, 1, 4)
        b = np.zeros((DEPTH, 2 * KT, P, FF_HALVES[0] * P), f)
        first = 0
        for h, n in enumerate(FF_HALVES):
            b[:, h * KT:(h + 1) * KT, :, 0:n * P] = w[:, :, :, first:first + n].reshape(DEPTH, KT, P, n * P)
            first += n
        return b

    def blocks(w):
        n = w.shape[2] // (2 * P)
        return w.reshape(DEPTH, KT, P, n, 2 * P).transpose(0, 3, 2, 1, 4).reshape(DEPTH, n, P, 2 * D)

    out["w_up1"], out["w_down1"] = up(a["w_ffn1_in"]), down(a["w_ffn1_out"])
    out["w_up2"], out["w_down2"] = up(a["w_ffn2_in"]), down(a["w_ffn2_out"])
    qk, g8, r16 = HEADS * DK, 2 * HEADS, a["w_gla_lr2"].shape[1]
    sizes = [qk, qk, D, D, g8, qk, qk, D, D, r16, D, D, 3 * D]
    mq, mk, mv, mo, mif, gq, gk, gv, gg, glr_, lx, ly, mg = np.split(a["w_in"], np.cumsum(sizes)[:-1], axis=2)
    order = []
    for q, k, v, o, br in ((mq, mk, mv, mo, 0), (gq, gk, gv, gg, 1)):
        for h in range(HEADS):
            c1, c2 = slice(h * DK, (h + 1) * DK), slice(h * DV, (h + 1) * DV)
            order += [q[..., c1], k[..., c1], v[..., c2], o[..., c2], mg[..., br * D + h * DV:br * D + (h + 1) * DV]]
    for j in range(KT // 2):
        c2 = slice(j * 2 * P, (j + 1) * 2 * P)
        order += [lx[..., c2], ly[..., c2], mg[..., 2 * D + j * 2 * P:2 * D + (j + 1) * 2 * P]]
    out["w_mix"] = blocks(np.concatenate(order, axis=2))
    gw = np.zeros((DEPTH, D, P), f)
    gw[:, :, 0:HEADS], gw[:, :, 32:32 + HEADS], gw[:, :, 64:80] = mif[..., :HEADS], mif[..., HEADS:], glr_
    out["w_gates"] = gw.reshape(DEPTH, KT, P, P).transpose(0, 2, 1, 3).reshape(DEPTH, P, GATE_W)
    out["w_o"] = blocks(a["w_out"])

    def feat(v):
        return v.reshape(DEPTH, -1, P).transpose(0, 2, 1)

    nxt = np.stack([a["norm_ffn1"][l + 1] if l + 1 < DEPTH else a["norm_final"] for l in range(DEPTH)])
    conv = a["w_conv"].reshape(DEPTH, 4 * D)
    per = np.concatenate([feat(v) for v in (a["norm_mix"], a["norm_ffn2"], nxt, a["g_ml_norm"], a["g_gla_norm"], conv,
                                            a["b_conv"], a["b_lru_a"], a["b_lru_i"], a["lru_lambda"],
                                            a["b_gla_gate"])], axis=2)
    out["vec"] = np.concatenate([per[l] for l in range(DEPTH)] + [a["norm_ffn1"][0].reshape(KT, P).T], axis=1)
    out["b_if"] = a["b_ml_if"].reshape(DEPTH, 2, HEADS).transpose(2, 0, 1)
    out["w_lr2"] = a["w_gla_lr2"].reshape(DEPTH, r16, HEADS, DK).transpose(0, 2, 1, 3)
    for n_, w in (("w_ra", a["w_lru_a"]), ("w_ri", a["w_lru_i"])):
        out[n_] = w.reshape(DEPTH, 2, KT // 2, P, P).transpose(0, 1, 3, 2, 4)
    s, t = np.arange(P)[:, None], np.arange(P)[None, :]
    c = np.zeros((P, 2 * P + P + NS + SEQS + N), f)
    c[:, 0:P], c[:, P:2 * P] = np.eye(P), 1
    c[:, 2 * P:3 * P] = np.where(s <= t, 0, NEG)
    s4, t4 = np.arange(NS)[:, None], np.arange(NS)[None, :]
    o = 3 * P
    c[0:NS, o:o + NS] = np.where((s4 <= t4) & (s4 // TS == t4 // TS), 0, NEG)
    c[0:NS, o + NS:o + NS + SEQS] = s4 // TS == np.arange(SEQS)[None, :]
    tok = np.arange(N)
    c[:, o + NS + SEQS:] = np.where(tok < T, tok % C != 0, (tok - T) % TS != 0)
    out["consts"] = c
    out["level_masks"] = np.stack([(s // (2 * h) == t // (2 * h)) & (s % (2 * h) < h) & (t % (2 * h) >= h)
                                   for h in LEVELS], axis=1).astype(np.int32)
    out["m0"] = a["state_mlstm_m"].transpose(2, 0, 1)
    out["c0"] = a["state_mlstm_C"].transpose(0, 2, 4, 1, 3)
    out["n0"] = a["state_mlstm_n"].transpose(0, 2, 3, 1)
    out["s0"] = a["state_gla_S"].transpose(0, 2, 3, 1, 4)
    out["h0"] = a["state_lru_h"].reshape(DEPTH, SEQS, KT, P).transpose(0, 3, 2, 1)
    out["conv0"] = a["state_lru_conv"].reshape(DEPTH, SEQS, 3, KT, P).transpose(0, 4, 3, 1, 2)
    return {k: np.ascontiguousarray(v) for k, v in out.items()}


_OUTS = {
    "o_y": (P, KT, N), "o_pc": (DEPTH, HEADS, P, DV + 1), "o_pm": (DEPTH, HEADS, 1), "o_ps": (DEPTH, HEADS, P, DV),
    "o_ph": (DEPTH, P, KT), "o_pconv": (DEPTH, P, KT, 3), "o_sc": (DEPTH, HEADS, P, SEQS, DV),
    "o_sn": (DEPTH, HEADS, P, SEQS), "o_sm": (DEPTH, HEADS, SEQS), "o_ss": (DEPTH, HEADS, P, SEQS, DV),
    "o_sh": (DEPTH, P, KT, SEQS), "o_sconv": (DEPTH, P, KT, SEQS, 3),
}


def kernel(**inputs):
    import numpy as np
    import concourse.bacc as bacc
    from concourse import mybir as mb
    from concourse.bass_utils import run_bass_kernel_spmd as run

    nc = bacc.Bacc("TRN2", target_bir_lowering=False, num_devices=1)
    arrays, args = {}, {}
    for name, v in _layout(inputs).items():
        arrays[f"in_{name}"] = v
        args[name] = nc.dram_tensor(f"in_{name}", v.shape, mb.dt.from_np(v.dtype), kind="ExternalInput").ap()
    for name, shape in _OUTS.items():
        args[name] = nc.dram_tensor(f"out_{name}", shape, mb.dt.float32, kind="ExternalOutput").ap()
    args["rows_dram"] = nc.dram_tensor("rows_scratch", (HEADS, 4 * N), mb.dt.float32, kind="Internal").ap()
    trunk(nc, **args)
    r = run(nc, [arrays], core_ids=[0]).results[0]
    o = {name: np.asarray(r[f"out_{name}"]) for name in _OUTS}

    y = o["o_y"].transpose(2, 1, 0).reshape(N, D)
    pc = o["o_pc"]
    got = (
        y[:T][None], y[T:].reshape(SEQS, TS, D),
        pc[..., :DV].transpose(0, 1, 3, 2)[:, None], pc[..., DV][:, None], o["o_pm"][:, None, :, 0],
        o["o_ps"][:, None], o["o_ph"].transpose(0, 2, 1).reshape(DEPTH, 1, D),
        o["o_pconv"].transpose(0, 3, 2, 1).reshape(DEPTH, 1, 3, D),
        o["o_sc"].transpose(0, 3, 1, 4, 2), o["o_sn"].transpose(0, 3, 1, 2), o["o_sm"].transpose(0, 2, 1),
        o["o_ss"].transpose(0, 3, 1, 2, 4), o["o_sh"].transpose(0, 3, 2, 1).reshape(DEPTH, SEQS, D),
        o["o_sconv"].transpose(0, 3, 4, 2, 1).reshape(DEPTH, SEQS, 3, D),
    )
    return tuple(np.ascontiguousarray(v) for v in got)
```
